# Optimizing a Trainium2 kernel written in Bass

```python
import math
import jax
import jax.numpy as jnp
from jax import lax
import numpy as np

D_MODEL = 1024
BATCH = 1
SEQ = 512
DEPTH = 1

N_HEADS = 8
HEAD_DIM = 64
N_KV = 2
HPG = N_HEADS // N_KV
CMP_STRIDE = 16
CMP_BLOCK = 2 * CMP_STRIDE
CMP_HIDDEN = 128
SLC_BLOCK = 64
N_SEL = 16
WINDOW = 512
Q_BLOCK = 128
REL_BUCKETS = 32
REL_MAX_DIST = 128
S5_WIDTH = 512
S5_GROUP = 16
S5_GROUPS = S5_WIDTH // S5_GROUP
S5_STATE = 64
S5_DT_MIN = 1e-3
S5_DT_MAX = 1e-1
N_EGROUPS = 8
EXPERTS_PER_GROUP = 8
N_EXPERTS = N_EGROUPS * EXPERTS_PER_GROUP
TOP_K_IN_GROUP = 2
D_EXPERT = 256
EXPERT_BLOCK = 128
DN_ALPHA = (2.0 * DEPTH) ** 0.25
DN_BETA = (8.0 * DEPTH) ** -0.25
LN_EPS = 1e-5
NEG_INF = -1e30
BIG = 1e9

ATTN_WIDTH = N_HEADS * HEAD_DIM
KV_WIDTH = N_KV * HEAD_DIM
KV_OFF = ATTN_WIDTH
NSA_GATE_OFF = KV_OFF + 6 * KV_WIDTH
S5_OFF = NSA_GATE_OFF + 3 * N_HEADS
MERGE_OFF = S5_OFF + S5_WIDTH
D_IN = MERGE_OFF + 2 * D_MODEL

kernel_name = 'hybrid_nsa_s5_hmoe_deepnorm'

def layer_norm(x, g, b):
    xf = x.astype(jnp.float32)
    mu = jnp.mean(xf, -1, keepdims=True)
    var = jnp.mean(jnp.square(xf - mu), -1, keepdims=True)
    return ((xf - mu) * lax.rsqrt(var + LN_EPS) * g.astype(jnp.float32) + b.astype(jnp.float32)).astype(x.dtype)

def t5_bucket(dist):
    n = jnp.maximum(dist, 0)
    max_exact = REL_BUCKETS // 2
    nf = jnp.maximum(n, 1).astype(jnp.float32)
    large = max_exact + (jnp.log(nf / max_exact) / math.log(REL_MAX_DIST / max_exact)
                         * (REL_BUCKETS - max_exact)).astype(jnp.int32)
    large = jnp.minimum(large, REL_BUCKETS - 1)
    return jnp.where(n < max_exact, n, large)

def masked_softmax(s, mask):
    p = jax.nn.softmax(jnp.where(mask, s, NEG_INF), axis=-1)
    return jnp.where(mask, p, 0.0)

def nsa_attention(q, kv, gates, rel_bias, cmp_pos, cmp_w1, cmp_b1, cmp_w2, cmp_b2):
    B, L = q.shape[:2]
    f32 = jnp.float32
    scale = HEAD_DIM ** -0.5
    qg = q.reshape(B, L, N_KV, HPG, HEAD_DIM).transpose(0, 2, 3, 1, 4)
    pos = jnp.arange(L)
    tbl = rel_bias.astype(f32)

    n_cmp = L // CMP_STRIDE - 1

    def compress(t, i):
        c = t.reshape(B, L // CMP_STRIDE, CMP_STRIDE, N_KV, HEAD_DIM)
        blk = jnp.concatenate([c[:, :-1], c[:, 1:]], axis=2)
        blk = blk + cmp_pos[i][None, None, :, None, :]
        blk = blk.transpose(0, 3, 1, 2, 4).reshape(B, N_KV, n_cmp, CMP_BLOCK * HEAD_DIM)
        hid = jax.nn.gelu(blk @ cmp_w1[i] + cmp_b1[i])
        return hid @ cmp_w2[i] + cmp_b2[i]

    kc = compress(kv[:, :, 0], 0)
    vc = compress(kv[:, :, 1], 1)
    cmp_start = jnp.arange(n_cmp) * CMP_STRIDE
    dist_c = pos[:, None] - (cmp_start + CMP_BLOCK - 1)[None, :]
    bias_c = tbl[t5_bucket(dist_c)].transpose(2, 0, 1).reshape(N_KV, HPG, L, n_cmp)
    s_c = jnp.einsum('bghqd,bgkd->bghqk', qg, kc).astype(f32) * scale + bias_c
    p_c = masked_softmax(s_c, dist_c >= 0)
    o_cmp = jnp.einsum('bghqk,bgkd->bghqd', p_c.astype(vc.dtype), vc)

    n_blk = L // SLC_BLOCK
    blk_ids = jnp.arange(n_blk)
    blk_start = blk_ids * SLC_BLOCK
    overlap = ((cmp_start[:, None] <= blk_start[None, :] + SLC_BLOCK - 1)
               & (cmp_start[:, None] + CMP_BLOCK - 1 >= blk_start[None, :])).astype(f32)
    imp = jnp.einsum('bghqk,kn->bgqn', p_c, overlap)
    cur = pos // SLC_BLOCK
    forced = (blk_ids[None, :] == 0) | (blk_ids[None, :] == cur[:, None]) | (blk_ids[None, :] == cur[:, None] - 1)
    valid = blk_start[None, :] <= pos[:, None]
    score = jnp.where(forced, BIG, jnp.where(valid, imp, -BIG))
    n_sel = min(N_SEL, n_blk)
    _, sel_idx = lax.top_k(score, n_sel)

    ks = kv[:, :, 2].transpose(0, 2, 1, 3).reshape(B, N_KV, n_blk, SLC_BLOCK, HEAD_DIM)
    vs = kv[:, :, 3].transpose(0, 2, 1, 3).reshape(B, N_KV, n_blk, SLC_BLOCK, HEAD_DIM)
    pad = ((0, 0), (0, 0), (WINDOW, 0), (0, 0))
    kw = jnp.pad(kv[:, :, 4].transpose(0, 2, 1, 3), pad)
    vw = jnp.pad(kv[:, :, 5].transpose(0, 2, 1, 3), pad)
    tbl_g = tbl.reshape(REL_BUCKETS, N_KV, HPG).transpose(1, 0, 2)
    bi = jnp.arange(B)[:, None, None, None]
    gi = jnp.arange(N_KV)[None, :, None, None]

    def query_block(c):
        q0 = c * Q_BLOCK
        qc = lax.dynamic_slice_in_dim(qg, q0, Q_BLOCK, axis=3)
        tq = q0 + jnp.arange(Q_BLOCK)
        idx = lax.dynamic_slice_in_dim(sel_idx, q0, Q_BLOCK, axis=2)
        kg = ks[bi, gi, idx]
        vg = vs[bi, gi, idx]
        kpos = idx[..., None] * SLC_BLOCK + jnp.arange(SLC_BLOCK)
        dist = tq[None, None, :, None, None] - kpos
        bias = tbl_g[gi[..., None], t5_bucket(dist)].transpose(0, 1, 5, 2, 3, 4)
        s = jnp.einsum('bghqd,bgqnsd->bghqns', qc, kg).astype(f32) * scale + bias
        s = s.reshape(B, N_KV, HPG, Q_BLOCK, n_sel * SLC_BLOCK)
        m = (dist >= 0).reshape(B, N_KV, 1, Q_BLOCK, n_sel * SLC_BLOCK)
        p = masked_softmax(s, m)
        o_s = jnp.einsum('bghqm,bgqmd->bghqd', p.astype(vg.dtype),
                         vg.reshape(B, N_KV, Q_BLOCK, n_sel * SLC_BLOCK, HEAD_DIM))
        kwc = lax.dynamic_slice_in_dim(kw, q0, Q_BLOCK + WINDOW, axis=2)
        vwc = lax.dynamic_slice_in_dim(vw, q0, Q_BLOCK + WINDOW, axis=2)
        kpos_w = q0 - WINDOW + jnp.arange(Q_BLOCK + WINDOW)
        dist_w = tq[:, None] - kpos_w[None, :]
        mask_w = (dist_w >= 0) & (dist_w < WINDOW) & (kpos_w[None, :] >= 0)
        bias_w = tbl[t5_bucket(dist_w)].transpose(2, 0, 1).reshape(N_KV, HPG, Q_BLOCK, Q_BLOCK + WINDOW)
        s_w = jnp.einsum('bghqd,bgkd->bghqk', qc, kwc).astype(f32) * scale + bias_w
        p_w = masked_softmax(s_w, mask_w)
        o_w = jnp.einsum('bghqk,bgkd->bghqd', p_w.astype(vwc.dtype), vwc)
        return o_s, o_w

    o_slc, o_win = lax.map(query_block, jnp.arange(L // Q_BLOCK))
    o_slc = o_slc.transpose(1, 0, 4, 2, 3, 5).reshape(B, L, N_HEADS, HEAD_DIM)
    o_win = o_win.transpose(1, 0, 4, 2, 3, 5).reshape(B, L, N_HEADS, HEAD_DIM)
    o_cmp = o_cmp.transpose(0, 3, 1, 2, 4).reshape(B, L, N_HEADS, HEAD_DIM)
    o = gates[..., 0:1] * o_cmp + gates[..., 1:2] * o_slc + gates[..., 2:3] * o_win
    return o.astype(q.dtype).reshape(B, L, ATTN_WIDTH)

def s5_layer(u, lam_re, lam_im, log_dt, b_re, b_im, c_re, c_im, d_skip):
    B, L, _ = u.shape
    f32 = jnp.float32
    uf = u.astype(f32).reshape(B, L, S5_GROUPS, S5_GROUP)
    dt = jnp.exp(log_dt.astype(f32))[:, None]
    lr, li = lam_re.astype(f32), lam_im.astype(f32)
    mag = jnp.exp(lr * dt)
    ab_re, ab_im = mag * jnp.cos(li * dt), mag * jnp.sin(li * dt)
    nr, ni = ab_re - 1.0, ab_im
    den = lr * lr + li * li
    fr, fi = (nr * lr + ni * li) / den, (ni * lr - nr * li) / den
    br, bim = b_re.astype(f32), b_im.astype(f32)
    bb_re = fr[..., None] * br - fi[..., None] * bim
    bb_im = fr[..., None] * bim + fi[..., None] * br
    bu_re = jnp.einsum('blgh,gph->blgp', uf, bb_re)
    bu_im = jnp.einsum('blgh,gph->blgp', uf, bb_im)
    a_re = jnp.broadcast_to(ab_re[None, None], (1, L, S5_GROUPS, S5_STATE))
    a_im = jnp.broadcast_to(ab_im[None, None], (1, L, S5_GROUPS, S5_STATE))

    def combine(e1, e2):
        a1r, a1i, b1r, b1i = e1
        a2r, a2i, b2r, b2i = e2
        return (a2r * a1r - a2i * a1i, a2r * a1i + a2i * a1r,
                a2r * b1r - a2i * b1i + b2r, a2r * b1i + a2i * b1r + b2i)

    _, _, xr, xi = lax.associative_scan(combine, (a_re, a_im, bu_re, bu_im), axis=1)
    y = (jnp.einsum('blgp,ghp->blgh', xr, c_re.astype(f32))
         - jnp.einsum('blgp,ghp->blgh', xi, c_im.astype(f32))
         + d_skip.astype(f32) * uf)
    return y.reshape(B, L, S5_WIDTH).astype(u.dtype)

def hier_moe(h, w_rg, b_rg, w_re, b_re, w_gate, w_up, w_down):
    B, L, D = h.shape
    N = B * L
    f32 = jnp.float32
    xt = h.reshape(N, D)
    tok_ids = jnp.arange(N)
    g_logits = (xt @ w_rg).astype(f32) + b_rg.astype(f32)
    g_prob = jax.nn.softmax(g_logits, -1)
    g_top = jnp.argmax(g_logits, -1)
    p_group = g_prob[tok_ids, g_top][:, None]
    e_logits = ((xt @ w_re).astype(f32) + b_re.astype(f32)).reshape(N, N_EGROUPS, EXPERTS_PER_GROUP)
    e_logits = e_logits[tok_ids, g_top]
    top_v, top_i = lax.top_k(e_logits, TOP_K_IN_GROUP)
    w = jax.nn.softmax(top_v, -1) * p_group
    expert = g_top[:, None].astype(jnp.int32) * EXPERTS_PER_GROUP + top_i
    A = N * TOP_K_IN_GROUP
    e_flat = expert.reshape(A)
    w_flat = w.reshape(A)
    tok = jnp.repeat(tok_ids, TOP_K_IN_GROUP)
    order = jnp.argsort(e_flat)
    e_s, tok_s, w_s = e_flat[order], tok[order], w_flat[order]
    counts = jnp.bincount(e_flat, length=N_EXPERTS)
    padded = (counts + EXPERT_BLOCK - 1) // EXPERT_BLOCK * EXPERT_BLOCK
    start = jnp.cumsum(counts) - counts
    pend = jnp.cumsum(padded)
    pstart = pend - padded
    dest = pstart[e_s] + (jnp.arange(A) - start[e_s])
    n_blocks = -(-A // EXPERT_BLOCK) + N_EXPERTS
    cap = n_blocks * EXPERT_BLOCK
    row_tok = jnp.full((cap,), N, jnp.int32).at[dest].set(tok_s)
    blk_expert = jnp.minimum(jnp.searchsorted(pend, jnp.arange(n_blocks) * EXPERT_BLOCK, side='right'),
                             N_EXPERTS - 1)
    x_pad = jnp.concatenate([xt, jnp.zeros((1, D), xt.dtype)], axis=0)

    def run_block(args):
        rows, e = args
        xb = x_pad[rows]
        hb = jax.nn.silu(xb @ w_gate[e]) * (xb @ w_up[e])
        return hb @ w_down[e]

    yb = lax.map(run_block, (row_tok.reshape(n_blocks, EXPERT_BLOCK), blk_expert))
    y_assign = yb.reshape(cap, D)[dest].astype(f32) * w_s[:, None]
    out = jax.ops.segment_sum(y_assign, tok_s, num_segments=N)
    return out.astype(h.dtype).reshape(B, L, D)

def setup_inputs(seed: int = 0) -> dict:
    key = jax.random.key(seed)
    ks = jax.random.split(key, 40)
    f32 = jnp.float32

    def nrm(k, shape, s):
        return jax.random.normal(k, shape, f32) * s

    Dp = DEPTH
    col_scale = np.ones((D_IN,), np.float32)
    for j in (1, 3, 5):
        col_scale[KV_OFF + j * KV_WIDTH: KV_OFF + (j + 1) * KV_WIDTH] = DN_BETA
    col_scale = jnp.asarray(col_scale)
    lam_im0 = jnp.broadcast_to(math.pi * jnp.arange(S5_STATE, dtype=f32), (Dp, S5_GROUPS, S5_STATE))
    return {
        'x': nrm(ks[0], (BATCH, SEQ, D_MODEL), 1.0),
        'rel_bias': nrm(ks[1], (REL_BUCKETS, N_HEADS), 0.1),
        'w_in': nrm(ks[2], (Dp, D_MODEL, D_IN), D_MODEL ** -0.5) * col_scale,
        'b_in': nrm(ks[3], (Dp, D_IN), 0.01),
        'cmp_pos': nrm(ks[4], (Dp, 2, CMP_BLOCK, HEAD_DIM), 0.1),
        'cmp_w1': nrm(ks[5], (Dp, 2, CMP_BLOCK * HEAD_DIM, CMP_HIDDEN), (CMP_BLOCK * HEAD_DIM) ** -0.5),
        'cmp_b1': nrm(ks[6], (Dp, 2, CMP_HIDDEN), 0.01),
        'cmp_w2': nrm(ks[7], (Dp, 2, CMP_HIDDEN, HEAD_DIM), CMP_HIDDEN ** -0.5),
        'cmp_b2': nrm(ks[8], (Dp, 2, HEAD_DIM), 0.01),
        'w_attn_up': nrm(ks[9], (Dp, ATTN_WIDTH, D_MODEL), ATTN_WIDTH ** -0.5) * DN_BETA,
        's5_lambda_re': -0.5 + nrm(ks[10], (Dp, S5_GROUPS, S5_STATE), 0.01),
        's5_lambda_im': lam_im0 + nrm(ks[11], (Dp, S5_GROUPS, S5_STATE), 0.01),
        's5_log_dt': jax.random.uniform(ks[12], (Dp, S5_GROUPS), f32, math.log(S5_DT_MIN), math.log(S5_DT_MAX)),
        's5_b_re': nrm(ks[13], (Dp, S5_GROUPS, S5_STATE, S5_GROUP), (2 * S5_GROUP) ** -0.5),
        's5_b_im': nrm(ks[14], (Dp, S5_GROUPS, S5_STATE, S5_GROUP), (2 * S5_GROUP) ** -0.5),
        's5_c_re': nrm(ks[15], (Dp, S5_GROUPS, S5_GROUP, S5_STATE), S5_STATE ** -0.5),
        's5_c_im': nrm(ks[16], (Dp, S5_GROUPS, S5_GROUP, S5_STATE), S5_STATE ** -0.5),
        's5_d': nrm(ks[17], (Dp, S5_GROUPS, S5_GROUP), 1.0),
        's5_w_val': nrm(ks[18], (Dp, S5_WIDTH, D_MODEL), S5_WIDTH ** -0.5) * DN_BETA,
        's5_w_gate': nrm(ks[19], (Dp, S5_WIDTH, D_MODEL), S5_WIDTH ** -0.5),
        's5_b_gate': nrm(ks[20], (Dp, D_MODEL), 0.01),
        'w_out': nrm(ks[21], (Dp, D_MODEL, D_MODEL), D_MODEL ** -0.5) * DN_BETA,
        'ln1_g': 1.0 + nrm(ks[22], (Dp, D_MODEL), 0.01),
        'ln1_b': nrm(ks[23], (Dp, D_MODEL), 0.01),
        'router_w_group': nrm(ks[24], (Dp, D_MODEL, N_EGROUPS), D_MODEL ** -0.5),
        'router_b_group': nrm(ks[25], (Dp, N_EGROUPS), 0.01),
        'router_w_expert': nrm(ks[26], (Dp, D_MODEL, N_EXPERTS), D_MODEL ** -0.5),
        'router_b_expert': nrm(ks[27], (Dp, N_EXPERTS), 0.01),
        'exp_w_gate': nrm(ks[28], (Dp, N_EXPERTS, D_MODEL, D_EXPERT), D_MODEL ** -0.5),
        'exp_w_up': nrm(ks[29], (Dp, N_EXPERTS, D_MODEL, D_EXPERT), D_MODEL ** -0.5) * DN_BETA,
        'exp_w_down': nrm(ks[30], (Dp, N_EXPERTS, D_EXPERT, D_MODEL), D_EXPERT ** -0.5) * DN_BETA,
        'ln2_g': 1.0 + nrm(ks[31], (Dp, D_MODEL), 0.01),
        'ln2_b': nrm(ks[32], (Dp, D_MODEL), 0.01),
    }

def reference(x, rel_bias, w_in, b_in, cmp_pos, cmp_w1, cmp_b1, cmp_w2, cmp_b2, w_attn_up,
              s5_lambda_re, s5_lambda_im, s5_log_dt, s5_b_re, s5_b_im, s5_c_re, s5_c_im, s5_d,
              s5_w_val, s5_w_gate, s5_b_gate, w_out, ln1_g, ln1_b,
              router_w_group, router_b_group, router_w_expert, router_b_expert,
              exp_w_gate, exp_w_up, exp_w_down, ln2_g, ln2_b):
    B, L, D = x.shape
    for l in range(DEPTH):
        proj = x @ w_in[l] + b_in[l]
        q = proj[..., :ATTN_WIDTH].reshape(B, L, N_HEADS, HEAD_DIM)
        kv = proj[..., KV_OFF:NSA_GATE_OFF].reshape(B, L, 6, N_KV, HEAD_DIM)
        nsa_g = jax.nn.sigmoid(proj[..., NSA_GATE_OFF:S5_OFF].astype(jnp.float32)).reshape(B, L, N_HEADS, 3)
        u = proj[..., S5_OFF:MERGE_OFF]
        merge = jax.nn.sigmoid(proj[..., MERGE_OFF:].astype(jnp.float32)).reshape(B, L, 2, D)
        y_a = nsa_attention(q, kv, nsa_g, rel_bias, cmp_pos[l], cmp_w1[l], cmp_b1[l],
                            cmp_w2[l], cmp_b2[l]) @ w_attn_up[l]
        y_s = s5_layer(u, s5_lambda_re[l], s5_lambda_im[l], s5_log_dt[l], s5_b_re[l], s5_b_im[l],
                       s5_c_re[l], s5_c_im[l], s5_d[l])
        z = jax.nn.gelu(y_s)
        y_b = (z @ s5_w_val[l]) * jax.nn.sigmoid(z @ s5_w_gate[l] + s5_b_gate[l])
        mixed = (merge[:, :, 0] * y_a + merge[:, :, 1] * y_b).astype(x.dtype)
        x = layer_norm(DN_ALPHA * x + mixed @ w_out[l], ln1_g[l], ln1_b[l])
        y_m = hier_moe(x, router_w_group[l], router_b_group[l], router_w_expert[l], router_b_expert[l],
                       exp_w_gate[l], exp_w_up[l], exp_w_down[l])
        x = layer_norm(DN_ALPHA * x + y_m, ln2_g[l], ln2_b[l])
    return x


_drawn_inputs = setup_inputs


def setup_inputs(seed=0):
    import zlib

    import numpy as np

    out = dict(_drawn_inputs(seed))
    spreads = {}
    factors = {'rel_bias': 8.0,
     'b_in': 8.0,
     'cmp_pos': 8.0,
     'cmp_w1': 4.396,
     'cmp_b1': 8.0,
     'cmp_w2': 3.304,
     'cmp_b2': 8.0,
     'w_attn_up': 2.806,
     's5_lambda_re': 64.0,
     's5_lambda_im': 64.0,
     's5_log_dt': 64.0,
     's5_b_re': 64.0,
     's5_b_im': 64.0,
     's5_c_re': 64.0,
     's5_c_im': 64.0,
     's5_w_gate': 3.49,
     's5_b_gate': 200.0,
     'ln1_g': 5.235,
     'ln1_b': 5.512,
     'router_b_group': 8.0,
     'router_b_expert': 8.0,
     'ln2_g': 189.549,
     'ln2_b': 181.745}
    for name, (base, spread) in spreads.items():
        noise = np.random.default_rng([zlib.crc32(name.encode()), seed]).standard_normal(out[name].shape)
        drawn = base * np.exp(spread * noise) if base else spread * noise
        out[name] = jnp.asarray(drawn.astype(out[name].dtype))
    for name, factor in factors.items():
        out[name] = (out[name] * factor).astype(out[name].dtype)
    return out
```

```python
import math
from contextlib import ExitStack

import numpy as np
import concourse.bass as bass
from concourse import mybir

P = 128
L = 512
D = 1024
KC = D // P
TT = L // P
HEADS, HD, NKV = 8, 64, 2
KV = NKV * HD
ATT = HEADS * HD
PAIRS = HEADS // 2
CS, CB, CH = 16, 32, 128
NCMP = L // CS - 1
BUCKETS, MAXDIST = 32, 128
SW, SH, SG, SP_ = 512, 16, 32, 64
GP = SG // 2
T8 = 8
NCH = L // T8
NE, NG, EPG, DE = 64, 8, 8, 256
BLK = 64
FORCED = 4

MAXB = 80
TBW = MAXB + 8
NSLOT = 4
EW = KC * 2 * DE + 2 * D
INVALID = 4096
ALPHA = 2.0 ** 0.25
EPS = 1e-5
NEG = 1e30
QS = -(HD ** -0.5)
VC = 2 * KV + 3 * HEADS
RC = NG + NE
CG = 48

F32 = mybir.dt.float32
U32 = mybir.dt.uint32
ALU = mybir.AluOpType
ACT = mybir.ActivationFunctionType
AX = mybir.AxisListType.X

BC_U, BC_CMP, BC_K, BC_Q, BC_M, BC_SG, BC_B1, BC_B2 = 0, 4, 6, 8, 12, 28, 36, 38
NBC = 40
ROW_V, ROW_R, ROW_B2, ROW_LN = 0, VC, VC + RC, VC + RC + HD
NRC = 3 * P + NE + 2 * TBW + 19
S5_LR, S5_LI, S5_DT, S5_BR, S5_BI, S5_CR, S5_CI = 0, 16, 32, 48, 304, 560, 816
NS5 = 1072
TWO_PI_PARTS = (6.28125, 0.0019350051879882812, 3.0199159819e-07)
MAGIC = 12582912.0


def build_kernel(nc, a):
    ctx = ExitStack()
    with ctx:
        def sb(name, shape, dt=F32):
            return ctx.enter_context(nc.sbuf_tensor(name, shape, dt))

        def sem(name):
            return ctx.enter_context(nc.semaphore(name))

        arena = sb("arena", [P, NSLOT * EW])
        reg_a = sb("reg_a", [P, 8192])
        reg_b = sb("reg_b", [P, 4096])
        xT = sb("xT", [P, KC * L])
        x1 = sb("x1", [P, TT * D])
        reg_u = sb("reg_u", [P, 4096])
        reg_o = sb("reg_o", [P, 3072])
        small = sb("small", [P, 980])
        ps = [ctx.enter_context(nc.psum_tensor(f"ps{i}", [P, 512], F32)) for i in range(8)]

        class Region:
            def __init__(self, t, at=0):
                self.t, self.at = t, at

            def take(self, n, rows=P):
                self.at += n
                return self.t[0:rows, self.at - n:self.at]

        u_dram = nc.dram_tensor("u_scratch", (SW, L), F32, kind="Internal").ap()
        y_dram = nc.dram_tensor("y_scratch", (SW, L), F32, kind="Internal").ap()
        WB = P + L
        shift_dram = nc.dram_tensor("shift_scratch", (P, HEADS, WB), F32, kind="Internal").ap()
        shift_c_dram = nc.dram_tensor("shift_c_scratch", (NCMP, HEADS, 2 * L), F32, kind="Internal").ap()
        x1_dram = nc.dram_tensor("x1_scratch", (L, D), F32, kind="Internal").ap()
        ye_dram = nc.dram_tensor("ye_scratch", (2 * 2 * L, D // 2), F32, kind="Internal").ap()

        sm = Region(small)
        eye = sm.take(P)
        bcol = sm.take(NBC)
        qbias = sm.take(4)
        w2dup = sm.take(2 * P).rearrange("p (i n) -> p i n", i=2)
        hid = sm.take(2 * 2 * CG).rearrange("p (i n) -> p i n", i=2)
        b2row = sm.take(HD)
        post = sm.take(2 * CB).rearrange("p (i s) -> p i s", i=2)
        posb = sm.take(2 * CB).rearrange("p (i s) -> p i s", i=2)
        s5d = sm.take(GP, 32)
        eyeh = sm.take(SH, 32)
        rtbl = sm.take(HEADS, 33)

        ra = Region(reg_a)
        qT = ra.take(PAIRS * L).rearrange("p (n t) -> p n t", n=PAIRS)
        kz = ra.take(8 * L).rearrange("p (b g h t) -> p b g h t", b=2, g=2, h=2)
        vg = ra.take(TT * VC).rearrange("p (t n) -> p t n", t=TT)
        vrow = ra.take(VC)
        kcz = ra.take(2 * P).rearrange("p (g n) -> p g n", g=2)
        vcz = ra.take(2 * P).rearrange("p (g n) -> p g n", g=2)

        ring = reg_b[:, :].rearrange("p (r n) -> p r n", r=4)
        xTc = xT[:, :].rearrange("p (c t) -> p c t", c=KC)
        uT = reg_u[:, 0:2048].rearrange("p (g n) -> p g n", g=4)
        ublk = reg_u[:, 2048:4096].rearrange("p (g c) -> p g c", g=SG)
        ypre = reg_u[:, 0:2048].rearrange("p (g c) -> p g c", g=SG)
        zT = reg_u[:, 2048:4096].rearrange("p (g n) -> p g n", g=4)
        oT = reg_o[:, 0:2048].rearrange("p (n t) -> p n t", n=PAIRS)
        blkz = reg_o[:, 0:CB * 2 * CG].rearrange("p (s n) -> p s n", s=CB)

        ar = Region(arena)
        bias_t = ar.take(4096)
        toep = ar.take(4096).rearrange("p (g n) -> p g n", g=SG)
        work = ar.take(4096)
        ca_re = ar.take(GP * 9 * SH).rearrange("p (g j h) -> p g j h", g=GP, j=9)
        ca_ni = ar.take(GP * 9 * SH).rearrange("p (g j h) -> p g j h", g=GP, j=9)
        w1l = ar.take(4096).rearrange("p (g n) -> p g n", g=2 * GP)
        rot = ar.take(2 * GP * 65).rearrange("p (i g c) -> p i g c", i=2, g=GP)
        decay = ar.take(GP * NCH).rearrange("p (g c) -> p g c", g=GP)

        biasT = bias_t.rearrange("p (h k) -> p h k", h=HEADS)
        s5r = Region(arena)
        prm = s5r.take(NS5)
        bb = s5r.take(2 * 256).rearrange("p (i g h) -> p i g h", i=2, g=GP)
        bbz = s5r.take(2 * GP * 32).rearrange("p (i g m) -> p i g m", i=2, g=GP)
        apow = s5r.take(2 * GP * 9).rearrange("p (i g j) -> p i g j", i=2, g=GP)
        sp = [s5r.take(GP) for _ in range(40)]
        w1t = x1[:, :].rearrange("p (i g n) -> p i g n", i=2, g=GP)
        kst = x1[0:32, 0:2048].rearrange("p (g n) -> p g n", g=GP)
        xz = x1[:, :].rearrange("p (i g n) -> p i g n", i=2, g=GP)
        onehot = work[0:33, 0:2048]
        rsb = w1l.rearrange("p g n -> p (g n)")[0:HEADS, 0:2048]

        at = Region(arena, 8192)
        pbuf = at.take(4 * 1280).rearrange("p (b n) -> p b n", b=4)
        ptbuf = at.take(4 * 1280).rearrange("p (b n) -> p b n", b=4)
        bias_c = at.take(TT * HEADS * CB).rearrange("p (t h j) -> p t h j", t=TT, h=HEADS)
        pc = at.take(TT * HEADS * 64).rearrange("p (t h j) -> p t h j", t=TT, h=HEADS)
        pcT = at.take(PAIRS * L).rearrange("p (n t) -> p n t", n=PAIRS)
        stat = at.take(256)
        nmax = stat[:, 0:16].rearrange("p (b t) -> p b t", b=4)
        rsum = stat[:, 16:32].rearrange("p (b t) -> p b t", b=4)
        fac = stat[:, 32:48].rearrange("p (b t) -> p b t", b=4)
        cmin = stat[:, 64:96].rearrange("p (t h) -> p t h", t=TT)
        csum = stat[:, 96:128].rearrange("p (t h) -> p t h", t=TT)
        cfac = stat[:, 128:160].rearrange("p (t h) -> p t h", t=TT)
        bias_e = reg_b[0:NCMP, 0:4096].rearrange("p (h t) -> p h t", h=HEADS)
        QOFF = [0, 128, 384, 768]
        KOFF = [0, 512, 896, 1152]
        gate = lambda h, b: vg[:, :, 2 * KV + 3 * h + b]
        z = reg_u[:, 0:2048].rearrange("p (g t) -> p g t", g=4)
        MW = 28 * P
        mid = [arena[:, 4096:4096 + MW], arena[:, 0:MW]]
        sg = arena[:, 8192:12288].rearrange("p (b i t) -> p b i t", b=2, i=4)
        mixT = reg_b[:, :].rearrange("p (c t) -> p c t", c=KC)
        w_out = reg_a[:, :].rearrange("p (c n) -> p c n", c=KC)
        x1t = x1[:, :].rearrange("p (t n) -> p t n", t=TT)
        ln1g, ln1b = xT[:, 0:D], xT[:, D:2 * D]
        xtr = xT[:, 2 * D:4 * D].rearrange("p (b c t) -> p b c t", b=2, c=KC)

        ru = Region(reg_u)
        rw = ru.take(KC * RC + 24)
        rrow = ru.take(RC)
        rconst = ru.take(NRC)
        tril, ones, iota_e = rconst[:, 0:P], rconst[:, P:2 * P], rconst[:, 2 * P:2 * P + NE]
        o = 2 * P + NE
        iota_all = rconst[:, o:o + TBW]
        iota_b, forced_b = rconst[0:NE, o:o + TBW], rconst[0:NE, o + TBW:o + 2 * TBW]
        o += 2 * TBW
        ecol, fcol, thr, jcol = (rconst[0:NE, o:o + 1], rconst[0:NE, o + 1:o + 2], rconst[0:NE, o + 2:o + 10],
                                 rconst[:, o + 10:o + 11])
        token_less, slot_row = rconst[:, o + 11:o + 19], rconst[:, o + 19:o + 19 + P]
        hot_slot = xT[:, 2 * D:3 * D].rearrange("p (q s) -> p q s", q=8)
        hot_blk = xT[:, 3 * D:3 * D + 8 * TBW].rearrange("p (q b) -> p q b", q=8)
        lg = ru.take(TT * RC).rearrange("p (t n) -> p t n", t=TT)
        em = ru.take(TT * NE).rearrange("p (t g e) -> p t g e", t=TT, g=NG)
        pick = ru.take(2 * TT * NE).rearrange("p (k t e) -> p k t e", k=2, t=TT)
        both = ru.take(TT * NE).rearrange("p (t e) -> p t e", t=TT)
        prod = ru.take(TT * NE).rearrange("p (t e) -> p t e", t=TT)
        rt = [ru.take(TT * 8).rearrange("p (t e) -> p t e", t=TT) for _ in range(8)]
        r4 = [ru.take(8).rearrange("p (k t) -> p k t", k=2) for _ in range(16)]
        wts = ru.take(8).rearrange("p (k t) -> p k t", k=2)
        ind = ru.take(2 * TBW)
        diag = ru.take(NE)
        u32 = lambda n, rows=P: ru.take(n, rows).bitcast(U32)
        lt, gidx, sidx, ids = u32(TBW), u32(TBW // 2), u32(TBW), u32(TBW, 1)
        gcol, scol = [u32(1) for _ in range(2)], [u32(1) for _ in range(4)]
        rtu = [u32(TT * 8).rearrange("p (t e) -> p t e", t=TT) for _ in range(2)]
        hi_u, lo_u = u32(8), u32(8)
        idf = ru.take(TBW, 1)
        lnst = ru.take(64)
        re_ = Region(reg_a)
        xg = [re_.take(D) for _ in range(2)]
        xgT = [re_.take(KC * P).rearrange("p (c t) -> p c t", c=KC) for _ in range(2)]
        gs = [re_.take(P) for _ in range(2)]
        hb = [re_.take(P) for _ in range(2)]
        hT = [re_.take(P) for _ in range(2)]
        yb = [re_.take(D // 2) for _ in range(4)]
        slots = [arena[:, EW * i:EW * (i + 1)] for i in range(NSLOT)]
        yt = arena[:, 0:8192].rearrange("p (t k n) -> p t k n", t=TT, k=2)

        s_x = sem("s_x"); s_const = sem("s_const"); s_oh = sem("s_oh"); s_prm = sem("s_prm")
        s_ring = [sem(f"s_ring{i}") for i in range(4)]
        s_ring_used = sem("s_ring_used")
        s_proj = sem("s_proj"); s_proj_out = sem("s_proj_out")
        s_kv = sem("s_kv"); s_blk = sem("s_blk"); s_hid = sem("s_hid"); s_gelu = sem("s_gelu")
        s_zero = sem("s_zero")
        s_rm = sem("s_rm"); s_rsb = sem("s_rsb"); s_rd = sem("s_rd")
        s_act = sem("s_act"); s_dve = sem("s_dve"); s_pool = sem("s_pool")
        s_dtexp = sem("s_dtexp"); s_ang = sem("s_ang"); s_trig = sem("s_trig"); s_dt = sem("s_dt")
        s_ud = sem("s_ud"); s_ublk = sem("s_ublk")
        s_bbz = sem("s_bbz"); s_ca = sem("s_ca"); s_w1t = sem("s_w1t")
        s_w1p = sem("s_w1p"); s_w1l = sem("s_w1l"); s_kmm = sem("s_kmm"); s_kst = sem("s_kst")
        s_toep = sem("s_toep"); s_s = sem("s_s"); s_xz0 = sem("s_xz0"); s_xz = sem("s_xz")
        s_prot = sem("s_prot")
        s_y = sem("s_y"); s_yev = sem("s_yev"); s_yd = sem("s_yd"); s_zl = sem("s_zl"); s_z = sem("s_z")
        s_v = sem("s_v"); s_vb = sem("s_vb"); s_vev = sem("s_vev")
        s_kc = sem("s_kc"); s_kcev = sem("s_kcev")
        s_vrow = sem("s_vrow")
        s_bt = sem("s_bt"); s_be = sem("s_be"); s_gate = sem("s_gate")
        s_bct = sem("s_bct"); s_bce = sem("s_bce")
        s_cs = sem("s_cs"); s_cd = sem("s_cd"); s_ce = sem("s_ce"); s_cb = sem("s_cb"); s_cf = sem("s_cf"); s_cm = sem("s_cm")
        s_pcz = sem("s_pcz"); s_ct = sem("s_ct"); s_cte = sem("s_cte")
        s_sc = sem("s_sc"); s_min = sem("s_min"); s_exp = sem("s_exp"); s_scl = sem("s_scl")
        s_tr = sem("s_tr"); s_pta = sem("s_pta"); s_ptd = sem("s_ptd"); s_pv = sem("s_pv"); s_ot = sem("s_ot")
        s_mid = [sem("s_mid0"), sem("s_mid1")]; s_midd = sem("s_midd")
        s_dm = sem("s_dm"); s_sig = sem("s_sig"); s_mix = sem("s_mix")
        s_wo = sem("s_wo"); s_xr = sem("s_xr"); s_ln1 = sem("s_ln1"); s_rc = sem("s_rc"); s_lr = sem("s_lr")
        s_pad = sem("s_pad"); s_womm = sem("s_womm"); s_var = sem("s_var"); s_std = sem("s_std")
        s_xt1 = sem("s_xt1"); s_xte = sem("s_xte"); s_lgm = sem("s_lgm"); s_lg = sem("s_lg")
        s_gd = sem("s_gd"); s_ge = sem("s_ge"); s_pick = sem("s_pick"); s_rank = sem("s_rank")
        s_nb = sem("s_nb"); s_st = sem("s_st"); s_base = sem("s_base"); s_ids = sem("s_ids")
        s_slot = sem("s_slot"); s_tbl = sem("s_tbl"); s_xs = sem("s_xs")
        s_idx = sem("s_idx"); s_idr = sem("s_idr"); s_x1d = sem("s_x1d")
        s_w = [sem(f"s_w{i}") for i in range(NSLOT)]
        s_xg0 = sem("s_xg0"); s_gi = sem("s_gi"); s_gst = sem("s_gst"); s_sst = sem("s_sst"); s_si = sem("s_si")
        s_g = [sem(f"s_g{i}") for i in range(2)]; s_sct = [sem(f"s_sct{i}") for i in range(4)]
        s_xt = sem("s_xt"); s_xe = sem("s_xe"); s_gu = sem("s_gu"); s_silu = sem("s_silu"); s_h = sem("s_h")
        s_ht = sem("s_ht"); s_he = sem("s_he"); s_dn = sem("s_dn"); s_ye = sem("s_ye"); s_moe = sem("s_moe")
        s_yt = [sem(f"s_yt{t}") for t in range(TT)]; s_ln2 = sem("s_ln2"); s_var2 = sem("s_var2")
        s_std2 = sem("s_std2"); s_row2 = sem("s_row2"); s_out = sem("s_out"); s_nrm = sem("s_nrm"); s_hat = sem("s_hat"); s_gain = sem("s_gain")

        block = ctx.enter_context(nc.Block())

        NRING = 20
        R_CMP, R_K, R_Q, R_W1 = 4, 6, 8, 12
        BANK = {R_CMP: 6, R_CMP + 1: 7}
        plain = [i for i in range(R_W1) if i not in BANK]

        @block.sync
        def _(sp_):
            sp_.dma_start(xT[:, :], a["x_t"]).then_inc(s_x, 16)
            for i in range(4):
                sp_.dma_start(ring[:, i, :], a["front_w"][i]).then_inc(s_ring[i], 16)
            for i in range(4, NRING):
                sp_.wait_ge(s_ring_used, i - 3)
                sp_.dma_start(ring[:, i % 4, :], a["front_w"][i]).then_inc(s_ring[i % 4], 16)
            sp_.wait_ge(s_ring_used, NRING)
            sp_.dma_start(reg_b[:, 0:KC * VC], a["w_v"]).then_inc(s_ring[0], 16)
            sp_.wait_ge(s_rd, 32)
            sp_.wait_ge(s_w1t, 1)
            sp_.wait_ge(s_kmm, 4)
            sp_.dma_start(biasT, bass.AP(shift_dram.tensor, P - 1, [[HEADS * WB - 1, P], [WB, HEADS], [1, L]])).then_inc(s_bt, 16)
            sp_.wait_ge(s_v, TT)
            sp_.dma_start(bias_e, bass.AP(shift_c_dram.tensor, L - (CB - 1),
                                          [[HEADS * 2 * L - CS, NCMP], [2 * L, HEADS], [1, L]])).then_inc(s_be, 16)
            sp_.wait_ge(s_y, 4)
            sp_.dma_start(mid[0], a["mid_w"][0]).then_inc(s_mid[0], 16)
            sp_.dma_start(x1[:, :], a["x_rows"]).then_inc(s_xr, 16)
            sp_.wait_ge(s_yd, 16 * T8)
            sp_.dma_start(zT, y_dram.rearrange("(g w) n -> w g n", g=4)).then_inc(s_zl, 16)
            sp_.wait_ge(s_min, 64)
            sp_.dma_start(mid[1], a["mid_w"][1]).then_inc(s_mid[1], 16)
            sp_.wait_ge(s_pv, 8)
            sp_.dma_start(reg_a[:, :], a["w_out"]).then_inc(s_wo, 16)
            for e in (2, 3):
                sp_.dma_start(slots[e], a["experts"][e * P:(e + 1) * P, :]).then_inc(s_w[e], 16)
            for d in range(2, KC):
                sp_.wait_ge(s_midd, d - 1)
                sp_.dma_start(mid[d % 2], a["mid_w"][d]).then_inc(s_mid[d % 2], 16)
            sp_.wait_ge(s_midd, KC)
            row = a["rows"]
            for n in range(2):
                sp_.dma_start(xT[:, n * D:(n + 1) * D],
                              row[0:1, ROW_LN + n * D:ROW_LN + (n + 1) * D].broadcast_to([P, D])).then_inc(s_lr, 16)
            sp_.dma_start(rw[:, 0:KC * RC], a["router_w"]).then_inc(s_rc, 16)
            sp_.dma_start(rconst, a["route_consts"]).then_inc(s_rc, 16)
            sp_.dma_start(rrow, row[0:1, ROW_R:ROW_R + RC].broadcast_to([P, RC])).then_inc(s_rc, 16)
            sp_.wait_ge(s_mix, 4 * KC)
            for e in (0, 1):
                sp_.dma_start(slots[e], a["experts"][e * P:(e + 1) * P, :]).then_inc(s_w[e], 16)
            for t in range(TT):
                sp_.wait_ge(s_ln1, t + 1)
                sp_.dma_start(x1_dram[t * P:(t + 1) * P, :], x1t[:, t, :]).then_inc(s_x1d, 16)
            for n in range(2):
                sp_.dma_start(xT[:, n * D:(n + 1) * D],
                              row[0:1, ROW_LN + (2 + n) * D:ROW_LN + (3 + n) * D].broadcast_to([P, D])).then_inc(s_row2, 16)
            sp_.wait_ge(s_idr, 1)
            extra = sp_.value_load(ids[0:1, MAXB:MAXB + 1], min_val=0, max_val=MAXB - 1 - FORCED)
            with sp_.Fori(1, MAXB // 4) as i:
                for k in range(4):
                    with sp_.If(4 * i + (k - FORCED) < extra):
                        e = sp_.value_load(ids[0:1, bass.ds(4 * i + k, 1)], min_val=0, max_val=(NE - 1) * P)
                        sp_.wait_ge(s_dn, 4 * i + (k - 3))
                        sp_.dma_start(slots[k], a["experts"][bass.ds(e, P), :]).then_inc(s_w[k], 16)
            sp_.wait_ge(s_moe, 1)
            ye = ye_dram.rearrange("(k t p j) n -> t p k (j n)", k=2, t=TT, p=P)
            for t in range(TT):
                sp_.dma_start(yt[:, t, :, :], ye[t]).then_inc(s_yt[t], 16)
            for t in range(TT):
                sp_.wait_ge(s_ln2, t + 1)
                sp_.dma_start(a["out"][t * P:(t + 1) * P, :], yt[:, t, 0, :]).then_inc(s_out, 16)
            sp_.wait_ge(s_out, 16 * TT)

        @block.tensor
        def _(pe):
            pe.wait_ge(s_x, 16)
            for i in range(R_W1):
                if i == R_CMP:
                    pe.wait_ge(s_oh, 32)
                    for n in range(4):
                        m = pe.matmul(ps[4 + n][0:HEADS, :], rtbl, onehot[:, n * 512:(n + 1) * 512], start=True, stop=True)
                    m.then_inc(s_rm, 1)
                pe.wait_ge(s_ring[i % 4], 16 * (i // 4 + 1))
                if i in BANK:
                    bank = BANK[i]
                    pe.wait_ge(s_rsb, 4)
                else:
                    n = plain.index(i)
                    bank = n % 4
                    if n >= 4:
                        pe.wait_ge(s_proj_out, n - 3)
                for c in range(KC):
                    m = pe.matmul(ps[bank][:, :], ring[:, i % 4, c * P:(c + 1) * P], xTc[:, c, :],
                                  start=(c == 0), stop=(c == KC - 1))
                m.then_inc(s_kv if i in BANK else s_proj, 1)
                pe.wait_ge(s_kv if i in BANK else s_proj, (i - R_CMP + 1) if i in BANK else n + 1)
                pe.nop().then_inc(s_ring_used, 1)
            for i in range(2):
                for r in range(4):
                    k = R_W1 + 4 * i + r
                    pe.wait_ge(s_ring[k % 4], 16 * (k // 4 + 1))
                    if r == 0:
                        pe.wait_ge(s_blk, i + 1)
                    for s in range(8):
                        m = pe.matmul(ps[4 + i][:, 0:2 * CG], ring[:, k % 4, s * P:(s + 1) * P],
                                      blkz[:, 8 * r + s, :], start=(r == 0 and s == 0), stop=(r == 3 and s == 7))
                    m.then_inc(s_ring_used, 1)
                pe.wait_ge(s_ring_used, R_W1 + 4 * (i + 1))
                pe.nop().then_inc(s_hid, 1)
            pe.wait_ge(s_w1t, 1)
            for n in range(8):
                if n >= 4:
                    pe.wait_ge(s_w1l, n - 3)
                elif n < 2:
                    pe.wait_ge(s_gelu, n + 1)
                for q in range(4):
                    j = 4 * n + q
                    m = pe.transpose(ps[4 + n % 4][:, q * P:(q + 1) * P], w1t[:, j % 2, j // 2, :], eye)
                m.then_inc(s_w1p, 1)
            pe.wait_ge(s_ca, 1)
            pe.wait_ge(s_bbz, 1)
            for g in range(GP):
                if g % 4 == 0:
                    pe.wait_ge(s_proj_out, len(plain))
                out = ps[g // 4][0:32, (g % 4) * P:(g % 4 + 1) * P]
                pe.matmul(out, bbz[:, 0, g, :], ca_re[:, g, 0:8, :], start=True, stop=False)
                m = pe.matmul(out, bbz[:, 1, g, :], ca_ni[:, g, 0:8, :], start=False, stop=True)
                if g % 4 == 3:
                    m.then_inc(s_kmm, 1)
            pe.wait_ge(s_w1l, 8)
            pe.wait_ge(s_ublk, 16 * T8)
            for g in range(GP):
                for ri in range(2):
                    for g2 in range(2):
                        m = pe.matmul(ps[4 + 2 * ri + g // 8][64 * g2:64 * g2 + 64, (g % 8) * NCH:(g % 8 + 1) * NCH],
                                      w1l[:, 2 * g + ri, 64 * g2:64 * g2 + 64], ublk[:, 2 * g + g2, :],
                                      start=True, stop=True)
            m.then_inc(s_s, 1)
            pe.wait_ge(s_ring[0], 16 * (NRING // 4 + 1))
            for t in range(TT):
                pe.wait_ge(s_kst, t + 1)
                for c in range(KC):
                    m = pe.matmul(ps[t][:, 0:VC], xTc[:, c, t * P:(t + 1) * P],
                                  reg_b[:, c * VC:(c + 1) * VC], start=(c == 0), stop=(c == KC - 1))
                m.then_inc(s_v, 1)
            pe.wait_ge(s_vev, 1)
            pe.matmul(ps[0][:, 0:2 * CG], w2dup[:, 0, :], hid[:, 0, :], start=True, stop=True)
            for g in range(2):
                m = pe.matmul(ps[0][0:NCMP, P + g * P:2 * P + g * P], hid[:, 1, g * CG:g * CG + NCMP], w2dup[:, 1, :],
                              start=True, stop=True)
            m.then_inc(s_kc, 1)
            pe.wait_ge(s_xz, 1)
            pe.wait_ge(s_vev, TT)
            pe.wait_ge(s_toep, 16 * 16)
            pe.wait_ge(s_kcev, 8)
            for g in range(GP):
                out = ps[g // 4][:, (g % 4) * P:(g % 4 + 1) * P]
                pe.matmul(out, ca_re[:, g, 1:9, :], xz[:, 0, g, :], start=True, stop=False)
                for g2 in range(2):
                    pe.matmul(out[:, 64 * g2:64 * g2 + 64], toep[:, 2 * g + g2, :], ublk[:, 2 * g + g2, :],
                              start=False, stop=False, skip_group_check=True)
                m = pe.matmul(out, ca_ni[:, g, 1:9, :], xz[:, 1, g, :], start=False, stop=True)
                if g % 4 == 3:
                    m.then_inc(s_y, 1)

            pe.wait_ge(s_be, 16)
            for t in range(TT):
                for h in range(HEADS):
                    m = pe.transpose(ps[4 + t // 2][:, (t % 2) * 256 + h * CB:(t % 2) * 256 + h * CB + NCMP],
                                     bias_e[:, h, t * P:(t + 1) * P], eye[0:NCMP, 0:NCMP])
                if t % 2:
                    m.then_inc(s_bct, 1)
            for t in range(TT):
                pe.wait_ge(s_yev, t + 1)
                for n in range(PAIRS):
                    m = pe.matmul(ps[t][:, n * P:(n + 1) * P], qT[:, n, t * P:(t + 1) * P], kcz[:, n // 2, :],
                                  start=True, stop=True)
                m.then_inc(s_cs, 1)

            def scores(u):
                n, b, h = u // 4, (u // 2) % 2, u % 2
                for k, tiles in enumerate(((3,), (2,), (0, 1))):
                    if u == 0:
                        pe.wait_ge(s_cd, k + 1)
                    else:
                        pe.wait_ge(s_min, 4 * u - 3 + (0, 1, 3)[k])
                    for q in tiles:
                        o = 0 if q != 1 else P
                        m = pe.matmul(ps[k][:, o:o + (q + 1) * P], qT[:, n, q * P:(q + 1) * P],
                                      kz[:, b, n // 2, h, 0:(q + 1) * P], start=True, stop=True)
                    m.then_inc(s_sc, 1)

            def transposes(u):
                pe.wait_ge(s_scl, 4 * (u + 1))
                for k, tiles in enumerate(((0,), (1,), (2, 3))):
                    if u == 0:
                        pe.wait_ge(s_bce if k else s_cd, 2 if k else 4)
                    elif k < 2:
                        pe.wait_ge(s_pta, 2 * u - 1 + k)
                    else:
                        pe.wait_ge(s_ptd, u)
                    o = 0
                    for kt in tiles:
                        for q in range(kt, TT):
                            m = pe.transpose(ps[3 + k][:, o:o + P], pbuf[:, u % 4, QOFF[q] + kt * P:QOFF[q] + (kt + 1) * P], eye)
                            o += P
                    m.then_inc(s_tr, 1)

            def compressed_transposes(t):
                pe.wait_ge(s_cm, t + 1)
                if t == 0:
                    pe.wait_ge(s_cd, 4)
                else:
                    pe.wait_ge(s_cte, t)
                for n in range(PAIRS):
                    m = pe.transpose(ps[3][:, n * P:(n + 1) * P], pc[:, t, 2 * n:2 * n + 2, :].rearrange("p h j -> p (h j)"), eye)
                m.then_inc(s_ct, 1)

            def values(w):
                n, b = w // 2, w % 2
                if w == 0:
                    pe.wait_ge(s_vb, 1)
                pe.wait_ge(s_pta, 4 * (w + 1))
                pe.wait_ge(s_ptd, 2 * (w + 1))
                if b == 0 and n >= 2:
                    pe.wait_ge(s_ot, n - 1)
                for kt in range(TT):
                    for h in range(2):
                        m = pe.matmul(ps[6 + n % 2][64 * h:64 * h + 64, kt * P:L],
                                      vg[:, kt, b * KV + (n // 2) * HD:b * KV + (n // 2 + 1) * HD],
                                      ptbuf[:, (2 * w + h) % 4, KOFF[kt]:KOFF[kt] + L - kt * P],
                                      start=(b == 0 and kt == 0), stop=False, skip_group_check=True)
                if b == 1:
                    if n == 0:
                        pe.wait_ge(s_cte, 4)
                    m = pe.matmul(ps[6 + n % 2][:, :], vcz[:, n // 2, :], pcT[:, n, :], start=False, stop=True,
                                  skip_group_check=True)
                m.then_inc(s_pv, 1)

            scores(0)
            for t in range(TT):
                compressed_transposes(t)
            scores(1)
            for u in range(2, 2 * 8 + 3):
                if u < 16:
                    scores(u)
                if u >= 5 and u % 2 == 1:
                    values((u - 5) // 2)
                if u - 2 < 16:
                    if u - 2 == 0:
                        pe.wait_ge(s_cte, 4)
                    transposes(u - 2)
            values(7)
            def mm(bank, w, o, rhs, nk):
                for c in range(nk):
                    m = pe.matmul(ps[bank][:, :], w[:, (o + c) * P:(o + c + 1) * P], rhs[:, c, :], start=(c == 0), stop=(c == nk - 1))
                m.then_inc(s_dm, 1)

            for d in range(KC):
                w = mid[d % 2]
                pe.wait_ge(s_mid[d % 2], 16 * (d // 2 + 1))
                for j, (o, rhs, nk) in enumerate(((0, xTc, 8), (8, xTc, 8), (24, z, 4), (16, oT, 4), (20, z, 4))):
                    bank = (5 * d + j) % 8
                    if 5 * d + j < 8:
                        if bank < 3:
                            pe.wait_ge(s_min, 64)
                        elif bank < 6:
                            pe.wait_ge(s_pta, 32)
                            pe.wait_ge(s_ptd, 16)
                        else:
                            pe.wait_ge(s_ot, 4)
                    else:
                        pd, pj = divmod(5 * d + j - 8, 5)
                        if pj < 3:
                            pe.wait_ge(s_sig, 3 * pd + pj + 1)
                        else:
                            pe.wait_ge(s_mix, 4 * pd + pj - 2)
                    if d == 0 and j == 2:
                        pe.wait_ge(s_z, 1)
                    if d == 0 and j == 3:
                        pe.wait_ge(s_ot, 4)
                    mm(bank, w, o, rhs, nk)
                pe.wait_ge(s_dm, 5 * (d + 1))
                pe.nop().then_inc(s_midd, 1)

            def project(t):
                if t == 0:
                    pe.wait_ge(s_wo, 16)
                    pe.wait_ge(s_mix, 4 * KC)
                for h in range(2):
                    for c in range(KC):
                        m = pe.matmul(ps[2 * t + h][:, :], mixT[:, c, t * P:(t + 1) * P], w_out[:, c, h * 512:(h + 1) * 512],
                                      start=(c == 0), stop=(c == KC - 1))
                m.then_inc(s_womm, 1)

            def x1_transposes(t):
                pe.wait_ge(s_ln1, t + 1)
                for c in range(KC):
                    m = pe.transpose(ps[2 * t + c // 4][:, (c % 4) * P:(c % 4 + 1) * P], x1t[:, t, c * P:(c + 1) * P], eye)
                m.then_inc(s_xt1, 1)

            def logits(t):
                if t == 0:
                    pe.wait_ge(s_rc, 16 * 3)
                    pe.wait_ge(s_pad, 1)
                pe.wait_ge(s_xte, 2 * (t + 1))
                for c in range(KC):
                    m = pe.matmul(ps[2 * t][:, 0:RC + 24], xtr[:, t % 2, c, :], rw[:, c * RC:c * RC + RC + 24],
                                  start=(c == 0), stop=(c == KC - 1))
                m.then_inc(s_lgm, 1)

            project(0)
            project(1)
            x1_transposes(0)
            project(2)
            logits(0)
            x1_transposes(1)
            project(3)
            logits(1)
            x1_transposes(2)
            logits(2)
            x1_transposes(3)
            logits(3)
            pe.wait_ge(s_pick, 1)
            for t in range(TT):
                for q in range(t + 1):
                    m = pe.matmul(ps[7][:, t * NE:(t + 1) * NE], ones if q < t else tril, both[:, q, :],
                                  start=(q == 0), stop=(q == t))
            for t in range(TT):
                m = pe.matmul(ps[5][0:NE, 0:1], both[:, t, :], ones[:, 0:1], start=(t == 0), stop=(t == TT - 1))
            m.then_inc(s_rank, 1)
            pe.wait_ge(s_nb, 1)
            pe.matmul(ps[4][0:NE, 0:1], tril[0:NE, 0:NE], r4[0][0:NE, 0, 1:2], start=True, stop=True).then_inc(s_st, 1)
            pe.wait_ge(s_base, 1)
            pe.matmul(ps[3][:, 0:NE], ones[0:NE, :], diag[0:NE, :], start=True, stop=True)
            pe.matmul(ps[3][0:1, 128:128 + TBW], ones[0:NE, 0:1], ind[0:NE, 0:TBW],
                      start=True, stop=True).then_inc(s_ids, 1)

            def turn_tokens(p, q):
                pe.wait_ge(s_g[q], 8 * p + (16 - 8 * q))
                if not isinstance(p, int) or p >= 1:
                    pe.wait_ge(s_xe, p)
                for c in range(KC):
                    m = pe.transpose(ps[c // 4][:, (c % 4) * P:(c % 4 + 1) * P], xg[q][:, c * P:(c + 1) * P], eye)
                m.then_inc(s_xt, 1)

            def gate_up(i, k):
                n = 4 * i + k
                pe.wait_ge(s_w[k], 16 * i + 16)
                pe.wait_ge(s_xe, 2 * i + (k // 2 + 1))
                if not isinstance(n, int) or n >= 2:
                    pe.wait_ge(s_h, n - 1)
                for c in range(KC):
                    for h in range(2):
                        m = pe.matmul(ps[2 + k % 2][64 * h:64 * h + 64, 0:DE], xgT[k // 2][:, c, BLK * (k % 2):BLK * (k % 2 + 1)],
                                      slots[k][:, c * 512 + h * DE:c * 512 + (h + 1) * DE],
                                      start=(c == 0), stop=(c == KC - 1))
                m.then_inc(s_gu, 1)

            def turn_hidden(n, k):
                pe.wait_ge(s_h, n + 1)
                if not isinstance(n, int) or n >= 2:
                    pe.wait_ge(s_he, n - 1)
                pe.transpose(ps[4 + k % 2][:, 0:P], hb[k % 2], eye).then_inc(s_ht, 1)

            def down(n, k):
                pe.wait_ge(s_he, n + 1)
                if not isinstance(n, int) or n >= 2:
                    pe.wait_ge(s_ye, n - 1)
                for h in range(2):
                    for j in range(2):
                        m = pe.matmul(ps[6 + k % 2][64 * j:64 * j + 64, :], hT[k % 2][:, 64 * h:64 * h + 64],
                                      slots[k][:, KC * 512 + h * D + j * 512:KC * 512 + h * D + (j + 1) * 512],
                                      start=(h == 0), stop=(h == 1))
                m.then_inc(s_dn, 1)

            def step(i, k):
                n = 4 * i + k
                gate_up(i, k)
                if not isinstance(n, int) or n >= 1:
                    turn_hidden(n - 1, (k + 3) % 4)
                if k % 2 == 0:
                    turn_tokens(2 * i + (k // 2 + 1), (k // 2 + 1) % 2)
                if not isinstance(n, int) or n >= 1:
                    down(n - 1, (k + 3) % 4)

            pe.wait_ge(s_slot, 1)
            for q in range(8):
                m = pe.matmul(ps[6][:, 0:TBW], hot_slot[:, q, :], hot_blk[:, q, :], start=(q == 0), stop=(q == 7))
            m.then_inc(s_tbl, 1)
            turn_tokens(0, 0)
            for k in range(4):
                step(0, k)
            pe.wait_ge(s_idr, 1)
            extra = pe.value_load(ids[0:1, MAXB:MAXB + 1], min_val=0, max_val=MAXB - 1 - FORCED)
            last = pe.value_load(ids[0:1, MAXB + 1:MAXB + 2], min_val=0, max_val=3)
            with pe.Fori(1, MAXB // 4) as i:
                for k in range(4):
                    with pe.If(4 * i + (k - FORCED) < extra):
                        step(i, k)
            for k in range(4):
                with pe.If(last == k):
                    turn_hidden(extra + (FORCED - 1), k)
                    down(extra + (FORCED - 1), k)

        @block.scalar
        def _(act):
            n_act = [0]

            def link(ins):
                n_act[0] += 1
                ins.then_inc(s_act, 1)
                act.wait_ge(s_act, n_act[0])

            act.wait_ge(s_prm, 16)
            act.activation(sp[0], prm[:, S5_DT:S5_DT + GP], ACT.Exp).then_inc(s_dt, 1)
            act.wait_ge(s_const, 16 * 7)
            link(act.mul(qbias, bcol[:, BC_Q:BC_Q + 4], QS))
            act.wait_ge(s_dtexp, 1)
            act.activation(sp[3], sp[2], ACT.Exp).then_inc(s_trig, 1)
            act.wait_ge(s_ang, 1)
            act.activation(arena_pair(s5r, sp, 8), arena_pair(s5r, sp, 6), ACT.Sin).then_inc(s_trig, 1)
            for n, i in enumerate(plain):
                act.wait_ge(s_proj, n + 1)
                src = ps[n % 4]
                if i < R_CMP:
                    act.activation(uT[:, i, :].rearrange("p (k c) -> p k c", k=T8),
                                   src[:, :].rearrange("p (c k) -> p k c", k=T8), ACT.Identity,
                                   bias=bcol[:, BC_U + i:BC_U + i + 1]).then_inc(s_proj_out, 1)
                    if i == R_CMP - 1:
                        act.wait_ge(s_proj_out, 4)
                        act.dma_start(u_dram.rearrange("(g w) n -> w g n", g=4), uT).then_inc(s_ud, 16)
                        act.wait_ge(s_rm, 1)
                        for n in range(4):
                            act.copy(rsb[:, n * 512:(n + 1) * 512], ps[4 + n][0:HEADS, :]).then_inc(s_rsb, 1)
                        act.wait_ge(s_rsb, 4)
                        act.dma_start(shift_dram.rearrange("p h w -> h p w"),
                                      rsb[:, 0:WB].unsqueeze(1).broadcast_to([HEADS, P, WB])).then_inc(s_rd, 16)
                        act.dma_start(shift_c_dram.rearrange("p h w -> h p w"),
                                      rsb[:, 2 * L:].unsqueeze(1).broadcast_to([HEADS, NCMP, 2 * L])).then_inc(s_rd, 16)
                        act.wait_ge(s_ud, 16)
                        ud = u_dram.rearrange("(g h) (k c) -> h k g c", h=SH, k=T8)
                        for k in range(T8):
                            act.dma_start(ublk[SH * k:SH * (k + 1), :, :], ud[:, T8 - 1 - k, :, :]).then_inc(s_ublk, 16)
                elif i < R_Q:
                    b = i - R_K
                    if b == 0:
                        act.wait_ge(s_zero, 2)
                    for g in range(2):
                        for h in range(2):
                            ins = act.activation(kz[64 * h:64 * h + 64, b, g, h, :], src[64 * g:64 * g + 64, :],
                                                 ACT.Identity, bias=bcol[64 * g:64 * g + 64, BC_K + b:BC_K + b + 1])
                            if g + h < 2:
                                link(ins)
                            else:
                                ins.then_inc(s_proj_out, 1)
                else:
                    act.activation(qT[:, i - R_Q, :], src[:, :], ACT.Identity,
                                   bias=qbias[:, i - R_Q:i - R_Q + 1], scale=QS).then_inc(s_proj_out, 1)
            for i in range(2):
                act.wait_ge(s_hid, i + 1)
                act.activation(hid[:, i, :], ps[4 + i][:, 0:2 * CG], ACT.Gelu_apprx_tanh,
                               bias=bcol[:, BC_B1 + i:BC_B1 + i + 1]).then_inc(s_gelu, 1)
            for n in range(8):
                act.wait_ge(s_w1p, n + 1)
                if n == 0:
                    act.wait_ge(s_rd, 32)
                act.copy(w1l[:, 4 * n:4 * n + 4, :], ps[4 + n % 4][:, :].rearrange("p (q n) -> p q n", q=4)).then_inc(s_w1l, 1)
            for n in range(4):
                act.wait_ge(s_kmm, n + 1)
                act.copy(kst[:, 4 * n:4 * n + 4, :], ps[n][0:32, :].rearrange("p (q n) -> p q n", q=4)).then_inc(s_kst, 1)
            act.wait_ge(s_kst, 5)
            act.wait_ge(s_zero, 6)
            for k in range(T8):
                for g2 in range(2):
                    act.dma_start(toep[SH * k:SH * (k + 1), g2:SG:2, (T8 - 1 - k) * SH:P],
                                  kst[SH * g2:SH * (g2 + 1), :, 0:(k + 1) * SH]).then_inc(s_toep, 16)
            for t in range(TT):
                act.wait_ge(s_v, t + 1)
                act.copy(vg[:, t, :], ps[t][:, 0:VC]).then_inc(s_vev, 1)
            act.wait_ge(s_kc, 1)
            act.wait_ge(s_zero, 6)
            for g in range(2):
                for h in range(2):
                    rows = slice(64 * h, 64 * h + 64)
                    act.activation(kcz[rows, g, 64 * h:64 * h + NCMP], ps[0][rows, g * CG:g * CG + NCMP],
                                   ACT.Identity, bias=bcol[rows, BC_B2:BC_B2 + 1]).then_inc(s_kcev, 1)
            for n in range(4):
                act.wait_ge(s_y, n + 1)
                act.copy(ypre[:, 8 * n:8 * n + 8, :], ps[n][:, :].rearrange("p (g c) -> p g c", c=NCH)).then_inc(s_yev, 1)
            act.wait_ge(s_yev, 4)
            yd = y_dram.rearrange("(g h) (k c) -> h k g c", h=SH, k=T8)
            for k in range(T8):
                act.dma_start(yd[:, k, :, :], ypre[SH * k:SH * (k + 1), :, :]).then_inc(s_yd, 16)

            act.wait_ge(s_vb, 1)
            act.activation(vg[:, :, 2 * KV:VC], vg[:, :, 2 * KV:VC], ACT.Sigmoid).then_inc(s_gate, 1)
            for n in range(2):
                act.wait_ge(s_bct, n + 1)
                if n == 0:
                    act.wait_ge(s_y, 4)
                act.copy(bias_c[:, 2 * n:2 * n + 2, :, 0:NCMP],
                         ps[4 + n][:, :].rearrange("p (t h j) -> p t h j", t=2, j=CB)[:, :, :, 0:NCMP]).then_inc(s_bce, 1)
            for t in range(TT):
                act.wait_ge(s_cd, t + 1)
                act.wait_ge(s_cb, t + 1)
                act.activation(pc[:, t, :, 0:NCMP], pc[:, t, :, 0:NCMP], ACT.Exp, scale=-1.0).then_inc(s_ce, 1)

            def exps(u):
                for k, q in enumerate((3, 2, 0, 1)):
                    act.wait_ge(s_min, 4 * u + k + 1)
                    tile = pbuf[:, u % 4, QOFF[q]:QOFF[q] + (q + 1) * P]
                    act.activation(tile, tile, ACT.Exp, bias=nmax[:, u % 4, q:q + 1], scale=-1.0,
                                   accum_out=rsum[:, u % 4, q:q + 1]).then_inc(s_exp, 1)

            def copies(u):
                for k in range(2):
                    act.wait_ge(s_tr, 3 * u + k + 1)
                    if u >= 4 and k == 0:
                        act.wait_ge(s_pv, (u - 4) // 2 + 1)
                    n = (L, 3 * P)[k]
                    act.copy(ptbuf[:, u % 4, KOFF[k]:KOFF[k] + n], ps[3 + k][:, 0:n]).then_inc(s_pta, 1)

            exps(0)
            for t in range(TT):
                act.wait_ge(s_ct, t + 1)
                act.copy(pcT[:, :, t * P:(t + 1) * P], ps[3][:, :].rearrange("p (n q) -> p n q", n=PAIRS)).then_inc(s_cte, 1)
            exps(1)
            for u in range(2, 18):
                if u < 16:
                    exps(u)
                copies(u - 2)
                if u >= 7 and (u - 7) % 4 == 0 and u < 16:
                    n = (u - 7) // 4
                    act.wait_ge(s_pv, 2 * n + 2)
                    act.copy(oT[:, n, :], ps[6 + n % 2][:, :]).then_inc(s_ot, 1)
            act.wait_ge(s_pv, 8)
            act.copy(oT[:, 3, :], ps[7][:, :]).then_inc(s_ot, 1)
            act.wait_ge(s_zl, 16)
            act.activation(z.rearrange("p g (c k) -> p g c k", k=T8), zT.rearrange("p g (k c) -> p g c k", k=T8),
                           ACT.Gelu_apprx_tanh).then_inc(s_z, 1)
            for d in range(KC):
                for j in range(3):
                    act.wait_ge(s_dm, 5 * d + j + 1)
                    if d >= 2 and j == 0:
                        act.wait_ge(s_mix, 4 * (d - 1))
                    b = bcol[:, BC_M + 2 * d + j:BC_M + 2 * d + j + 1] if j < 2 else bcol[:, BC_SG + d:BC_SG + d + 1]
                    act.activation(sg[:, d % 2, j, :], ps[(5 * d + j) % 8][:, :], ACT.Sigmoid, bias=b).then_inc(s_sig, 1)

            for t in range(TT):
                act.wait_ge(s_var, t + 1)
                act.activation(lnst[:, 32 + t:33 + t], lnst[:, 8 * t + 1:8 * t + 2], ACT.Sqrt).then_inc(s_std, 1)
                act.wait_ge(s_xt1, t + 1)
                if t == 0:
                    act.wait_ge(s_midd, KC)
                if t >= 2:
                    act.wait_ge(s_lgm, t - 1)
                for h in range(2):
                    act.copy(xtr[:, t % 2, 4 * h:4 * h + 4, :],
                             ps[2 * t + h][:, :].rearrange("p (c n) -> p c n", c=4)).then_inc(s_xte, 1)
            act.wait_ge(s_gd, 1)
            act.activation(rt[0], rt[0], ACT.Exp).then_inc(s_ge, 1)
            act.wait_ge(s_gd, 2)
            act.activation(r4[1][:, 0, :], r4[1][:, 0, :], ACT.Exp).then_inc(s_ge, 1)
            act.wait_ge(s_x1d, 16 * TT)
            act.wait_ge(s_xt1, TT)
            act.mul(x1t, x1t, ALPHA).then_inc(s_xs, 1)

            def silu(n, k):
                act.wait_ge(s_gu, n + 1)
                if not isinstance(n, int) or n >= 2:
                    act.wait_ge(s_h, n - 1)
                act.activation(gs[k % 2], ps[2 + k % 2][:, 0:P], ACT.Silu).then_inc(s_silu, 1)

            def result(n, k):
                act.wait_ge(s_dn, n + 1)
                if not isinstance(n, int) or n >= 4:
                    act.wait_ge(s_sct[k], 4 * n - 4 * k)
                act.copy(yb[k], ps[6 + k % 2][:, :]).then_inc(s_ye, 1)

            def step(i, k):
                n = 4 * i + k
                silu(n, k)
                if not isinstance(n, int) or n >= 1:
                    result(n - 1, (k + 3) % 4)

            for k in range(4):
                step(0, k)
            act.wait_ge(s_idr, 1)
            extra = act.value_load(ids[0:1, MAXB:MAXB + 1], min_val=0, max_val=MAXB - 1 - FORCED)
            last = act.value_load(ids[0:1, MAXB + 1:MAXB + 2], min_val=0, max_val=3)
            with act.Fori(1, MAXB // 4) as i:
                for k in range(4):
                    with act.If(4 * i + (k - FORCED) < extra):
                        step(i, k)
            for k in range(4):
                with act.If(last == k):
                    result(extra + (FORCED - 1), k)
            for j in range(TT + 1):
                if j < TT:
                    act.wait_ge(s_var2, j + 1)
                    act.activation(lnst[:, 32 + j:33 + j], lnst[:, 8 * j + 1:8 * j + 2], ACT.Sqrt).then_inc(s_std2, 1)
                if j >= 1:
                    t = j - 1
                    act.wait_ge(s_nrm, t + 1)
                    act.activation(yt[:, t, 1, :], yt[:, t, 0, :], ACT.Identity, bias=lnst[:, 52 + t:53 + t],
                                   scale=lnst[:, 36 + t:37 + t]).then_inc(s_hat, 1)

        @block.vector
        def _(dve):
            n_dve = [0]

            def link(ins):
                n_dve[0] += 1
                ins.then_inc(s_dve, 1)
                dve.wait_ge(s_dve, n_dve[0])

            def put(ins):
                n_dve[0] += 1
                ins.then_inc(s_dve, 1)

            def tt(out, x, y, op):
                return dve.tensor_tensor(out, x, y, op)

            def cmul(ore, oim, ar_, ai, br, bi, tmp):
                put(tt(tmp[0], ar_, br, ALU.mult))
                put(tt(tmp[1], ai, bi, ALU.mult))
                put(tt(tmp[2], ar_, bi, ALU.mult))
                link(tt(tmp[3], ai, br, ALU.mult))
                put(tt(ore, tmp[0], tmp[1], ALU.subtract))
                link(tt(oim, tmp[2], tmp[3], ALU.add))

            lr, li = prm[:, S5_LR:S5_LR + GP], prm[:, S5_LI:S5_LI + GP]
            dt, th, lrd, mag, k_, r_ = sp[0], sp[1], sp[2], sp[3], sp[4], sp[5]
            dve.wait_ge(s_prm, 16)
            dve.wait_ge(s_dt, 1)
            dve.tensor_tensor(lrd, lr, dt, ALU.mult).then_inc(s_dtexp, 1)
            link(tt(th, li, dt, ALU.mult))
            link(dve.tensor_scalar(k_, th, 1.0 / (2 * math.pi), MAGIC, ALU.mult, ALU.add))
            link(dve.tensor_scalar(k_, k_, MAGIC, None, ALU.subtract))
            src = th
            for part in TWO_PI_PARTS:
                link(dve.scalar_tensor_tensor(r_, k_, -part, src, ALU.mult, ALU.add))
                src = r_
            link(dve.tensor_scalar(sp[6], r_, 3.1415925, -3.1415925, ALU.min, ALU.max))
            link(dve.scalar_tensor_tensor(r_, sp[6], -1.0, sp[6], ALU.mult, ALU.max))
            dve.tensor_scalar(sp[7], r_, -1.0, math.pi / 2, ALU.mult, ALU.add).then_inc(s_ang, 1)
            put(tt(sp[10], lr, lr, ALU.mult))
            link(tt(sp[11], li, li, ALU.mult))
            link(tt(sp[10], sp[10], sp[11], ALU.add))
            link(dve.reciprocal(sp[11], sp[10]))
            dve.wait_ge(s_const, 16 * 7)
            link(tt(posb, post, bcol[:, BC_CMP:BC_CMP + 2].unsqueeze(2).broadcast_to([P, 2, CB]), ALU.add))
            dve.wait_ge(s_trig, 2)
            sin_, cos_ = sp[8], sp[9]
            put(dve.memset(apow[:, 0, :, 0:1], 1.0))
            put(dve.memset(apow[:, 1, :, 0:1], 0.0))
            put(dve.memset(rot[:, 0, :, 0:1], 1.0))
            link(dve.memset(rot[:, 1, :, 0:1], 0.0))
            are, aim = apow[:, 0, :, 1], apow[:, 1, :, 1]
            put(tt(are, mag, cos_, ALU.mult))
            link(tt(aim, mag, sin_, ALU.mult))
            link(dve.tensor_scalar(sp[12], are, 1.0, None, ALU.subtract))
            put(tt(sp[13], sp[12], lr, ALU.mult))
            put(tt(sp[14], aim, li, ALU.mult))
            put(tt(sp[15], aim, lr, ALU.mult))
            link(tt(sp[16], sp[12], li, ALU.mult))
            put(tt(sp[13], sp[13], sp[14], ALU.add))
            link(tt(sp[15], sp[15], sp[16], ALU.subtract))
            put(tt(sp[17], sp[13], sp[11], ALU.mult))
            link(tt(sp[18], sp[15], sp[11], ALU.mult))
            tmp = [x1[:, 1024 * i:1024 * (i + 1)] for i in range(4)]
            t3 = [t[:, 0:256].rearrange("p (g h) -> p g h", g=GP) for t in tmp]
            bre = prm[:, S5_BR:S5_BR + 256].rearrange("p (g h) -> p g h", g=GP)
            bim = prm[:, S5_BI:S5_BI + 256].rearrange("p (g h) -> p g h", g=GP)
            fre = sp[17].unsqueeze(2).broadcast_to([P, GP, SH])
            fim = sp[18].unsqueeze(2).broadcast_to([P, GP, SH])
            cmul(bb[:, 0], bb[:, 1], fre, fim, bre, bim, t3)
            dve.wait_ge(s_zero, 2)
            for g2 in range(2):
                rows = slice(64 * g2, 64 * g2 + 64)
                ins = dve.tensor_copy(bbz[rows, :, :, SH * g2:SH * (g2 + 1)], bb[rows, :, :, :])
                put(ins) if g2 == 0 else ins.then_inc(s_bbz, 1)
            for n in (1, 2, 4):
                t = [x[:, 0:GP * n].rearrange("p (g j) -> p g j", g=GP) for x in tmp]
                cmul(apow[:, 0, :, n + 1:2 * n + 1], apow[:, 1, :, n + 1:2 * n + 1],
                     apow[:, 0, :, 1:n + 1], apow[:, 1, :, 1:n + 1],
                     apow[:, 0, :, n:n + 1].broadcast_to([P, GP, n]), apow[:, 1, :, n:n + 1].broadcast_to([P, GP, n]), t)

            def cmp_block(i):
                dve.wait_ge(s_kv, i + 1)
                if i == 0:
                    dve.wait_ge(s_zero, 3)
                else:
                    dve.wait_ge(s_hid, 1)
                for g in range(2):
                    rows = slice(64 * g, 64 * g + 64)
                    full = ps[6 + i][rows, :]
                    src = bass.AP(full.tensor, full.offset, [list(full.ap[0]), [1, CB], [CS, NCMP]])
                    ins = dve.tensor_tensor(blkz[rows, :, g * CG:g * CG + NCMP], src,
                                            posb[rows, i, :].unsqueeze(2).broadcast_to([64, CB, NCMP]), ALU.add)
                    put(ins) if g == 0 else ins.then_inc(s_blk, 1)
                dve.wait_ge(s_dve, n_dve[0])

            def w_matrices():
                ce = x1[:, 0:GP * 9 * SH].rearrange("p (g j h) -> p g j h", g=GP, j=9)
                sh = [P, GP, 9, SH]
                cre = prm[:, S5_CR:S5_CR + 256].rearrange("p (g h) -> p g h", g=GP).unsqueeze(2).broadcast_to(sh)
                cim = prm[:, S5_CI:S5_CI + 256].rearrange("p (g h) -> p g h", g=GP).unsqueeze(2).broadcast_to(sh)
                pre, pim = (apow[:, i].unsqueeze(3).broadcast_to(sh) for i in range(2))
                put(tt(ca_re, cre, pre, ALU.mult))
                put(tt(ca_ni, cre, pim, ALU.mult))
                link(tt(ce, cim, pim, ALU.mult))
                link(tt(ca_re, ca_re, ce, ALU.subtract))
                link(tt(ce, cim, pre, ALU.mult))
                flat = [x.rearrange("p g j h -> p (g j h)") for x in (ca_ni, ce)]
                dve.scalar_tensor_tensor(flat[0], flat[0], -1.0, flat[1], ALU.mult, ALU.subtract).then_inc(s_ca, 1)
                dve.wait_ge(s_ca, 1)
                sh = [P, GP, T8, SH]
                w = [w1t[:, i].rearrange("p g (k h) -> p g k h", k=T8) for i in range(2)]
                tm = work[:, 0:2048].rearrange("p (g k h) -> p g k h", g=GP, k=T8)
                tm2 = work[:, 2048:4096].rearrange("p (g k h) -> p g k h", g=GP, k=T8)
                pre, pim = (apow[:, i, :, 0:T8].unsqueeze(3).broadcast_to(sh) for i in range(2))
                bbr, bbi = (bb[:, i].unsqueeze(2).broadcast_to(sh) for i in range(2))
                dve.wait_ge(s_rm, 1)
                put(tt(w[0], pre, bbr, ALU.mult))
                put(tt(tm, pim, bbi, ALU.mult))
                put(tt(w[1], pre, bbi, ALU.mult))
                link(tt(tm2, pim, bbr, ALU.mult))
                put(tt(w[0], w[0], tm, ALU.subtract))
                link(tt(w[1], w[1], tm2, ALU.add))
                dve.nop().then_inc(s_w1t, 1)

            cmp_block(0)
            cur = (cos_, sin_)
            t = [x[:, 0:GP] for x in tmp]
            for n in range(3):
                nxt = (rot[:, 0, :, 1], rot[:, 1, :, 1]) if n == 2 else (sp[20 + 2 * n], sp[21 + 2 * n])
                cmul(nxt[0], nxt[1], cur[0], cur[1], cur[0], cur[1], t)
                cur = nxt
            for n in (1, 2, 4, 8, 16, 32):
                t = [x[:, 0:GP * n].rearrange("p (g j) -> p g j", g=GP) for x in tmp]
                cmul(rot[:, 0, :, n + 1:2 * n + 1], rot[:, 1, :, n + 1:2 * n + 1],
                     rot[:, 0, :, 1:n + 1], rot[:, 1, :, 1:n + 1],
                     rot[:, 0, :, n:n + 1].broadcast_to([P, GP, n]), rot[:, 1, :, n:n + 1].broadcast_to([P, GP, n]), t)
            link(tt(sp[26], mag, mag, ALU.mult))
            link(tt(sp[27], sp[26], sp[26], ALU.mult))
            link(tt(sp[28], sp[27], sp[27], ALU.mult))
            link(dve.tensor_copy(decay, sp[28].unsqueeze(2).broadcast_to([P, GP, NCH])))
            link(dve.memset(decay[:, :, 0:1], 0.0))
            w_matrices()
            cmp_block(1)
            dve.wait_ge(s_kst, 4)
            sk = work[0:32, 0:256].rearrange("p (g h) -> p g h", g=GP)
            link(tt(sk, s5d.unsqueeze(2).broadcast_to([32, GP, SH]), eyeh.unsqueeze(1).broadcast_to([32, GP, SH]), ALU.mult))
            dve.tensor_tensor(kst[:, :, 0:SH], kst[:, :, 0:SH], sk, ALU.add).then_inc(s_kst, 1)
            dve.wait_ge(s_kst, 5)
            dve.wait_ge(s_s, 1)
            half = lambda t, i: t[:, 512 * i:512 * (i + 1)].rearrange("p (g c) -> p g c", g=8)
            w4 = [work[:, 1024 * i:1024 * (i + 1)] for i in range(4)]
            rc = [[rot[:, i, 8 * h:8 * h + 8, 0:NCH] for h in range(2)] for i in range(2)]
            sps = [[ps[4 + 2 * i + h][:, :].rearrange("p (g c) -> p g c", g=8) for h in range(2)] for i in range(2)]
            for h in range(2):
                put(tt(half(w4[0], h), sps[0][h], rc[0][h], ALU.mult))
                put(tt(half(w4[1], h), sps[1][h], rc[1][h], ALU.mult))
                put(tt(half(w4[2], h), sps[1][h], rc[0][h], ALU.mult))
                link(tt(half(w4[3], h), sps[0][h], rc[1][h], ALU.mult))
            put(tt(w4[0], w4[0], w4[1], ALU.add))
            link(tt(w4[2], w4[2], w4[3], ALU.subtract))
            dec = decay.rearrange("p g c -> p (g c)")
            put(dve.tensor_tensor_scan(w4[1], dec, w4[0], 0.0, ALU.mult, ALU.add))
            link(dve.tensor_tensor_scan(w4[3], dec, w4[2], 0.0, ALU.mult, ALU.add))
            g3 = lambda t: t.rearrange("p (g c) -> p g c", g=GP)
            rr, rim = rot[:, 0, :, 0:NCH], rot[:, 1, :, 0:NCH]
            put(tt(g3(w4[0]), g3(w4[1]), rr, ALU.mult))
            link(tt(g3(w4[2]), g3(w4[3]), rim, ALU.mult))
            dve.wait_ge(s_xz0, 1)

            def to_xz(i, op):
                for g2 in range(2):
                    rows = slice(64 * g2, 64 * g2 + 64)
                    put(tt(xz[rows, i, :, NCH * g2 + 1:NCH * (g2 + 1)], g3(w4[0])[rows, :, 0:NCH - 1],
                           g3(w4[2])[rows, :, 0:NCH - 1], op))
                dve.wait_ge(s_dve, n_dve[0])

            to_xz(0, ALU.subtract)
            put(tt(g3(w4[0]), g3(w4[1]), rim, ALU.mult))
            link(tt(g3(w4[2]), g3(w4[3]), rr, ALU.mult))
            to_xz(1, ALU.add)
            dve.nop().then_inc(s_xz, 1)
            dve.wait_ge(s_kcev, 4)
            for g in range(2):
                for h in range(2):
                    dve.tensor_tensor(vcz[64 * h:64 * h + NCMP, g, 64 * h:64 * h + 64],
                                      ps[0][0:NCMP, P + g * P:P + g * P + HD], b2row[0:NCMP, :], ALU.add).then_inc(s_kcev, 1)
            dve.wait_ge(s_vrow, 16)
            dve.wait_ge(s_vev, TT)
            dve.tensor_tensor(vg, vg, vrow.unsqueeze(1).broadcast_to([P, TT, VC]), ALU.add).then_inc(s_vb, 1)

            dve.wait_ge(s_bce, 2)
            dve.wait_ge(s_y, 4)
            dve.wait_ge(s_pcz, 1)
            wide = [P, HEADS, NCMP]
            for t in range(TT):
                dve.wait_ge(s_cs, t + 1)
                tile = pc[:, t, :, 0:NCMP]
                dve.tensor_tensor(tile, ps[t][:, :].rearrange("p (h j) -> p h j", h=HEADS)[:, :, 0:NCMP],
                                  bias_c[:, t, :, 0:NCMP], ALU.add).then_inc(s_cd, 1)
                dve.wait_ge(s_cd, t + 1)
                link(dve.tensor_reduce(cmin[:, t, :], tile, AX, ALU.min))
                dve.tensor_tensor(tile, tile, cmin[:, t, :].unsqueeze(2).broadcast_to(wide), ALU.subtract).then_inc(s_cb, 1)

            def minima(u):
                n, b, h = u // 4, (u // 2) % 2, u % 2
                for k, q in enumerate((3, 2, 0, 1)):
                    dve.wait_ge(s_sc, 3 * u + min(k, 2) + 1)
                    if k == 0 and u >= 4:
                        dve.wait_ge(s_tr, 3 * (u - 3))
                    o = 0 if q != 1 else P
                    w = (q + 1) * P
                    dve.tensor_tensor_reduce(out=pbuf[:, u % 4, QOFF[q]:QOFF[q] + w], in0=ps[min(k, 2)][:, o:o + w],
                                             in1=biasT[:, 2 * n + h, L - w:L], scale=1.0, scalar=3e38, op0=ALU.add,
                                             op1=ALU.min, accum_out=nmax[:, u % 4, q:q + 1]).then_inc(s_min, 1)

            def scales(u):
                n, b, h = u // 4, (u // 2) % 2, u % 2
                dve.wait_ge(s_exp, 4 * (u + 1))
                link(dve.reciprocal(fac[:, u % 4, :], rsum[:, u % 4, :]))
                link(tt(fac[:, u % 4, :], fac[:, u % 4, :], gate(2 * n + h, 1 + b), ALU.mult))
                for q in range(TT):
                    tile = pbuf[:, u % 4, QOFF[q]:QOFF[q] + (q + 1) * P]
                    dve.tensor_scalar(tile, tile, fac[:, u % 4, q:q + 1], None, ALU.mult).then_inc(s_scl, 1)

            def copies(u):
                dve.wait_ge(s_tr, 3 * (u + 1))
                if u >= 4:
                    dve.wait_ge(s_pv, (u - 4) // 2 + 1)
                dve.tensor_copy(ptbuf[:, u % 4, KOFF[2]:1280], ps[5][:, 0:3 * P]).then_inc(s_ptd, 1)

            dve.wait_ge(s_gate, 1)
            dve.wait_ge(s_bt, 16)
            minima(0)
            for t in range(TT):
                dve.wait_ge(s_ce, t + 1)
                tile = pc[:, t, :, 0:NCMP]
                link(dve.tensor_reduce(csum[:, t, :], tile, AX, ALU.add))
                link(dve.reciprocal(csum[:, t, :], csum[:, t, :]))
                link(tt(cfac[:, t, :], csum[:, t, :], vg[:, t, 2 * KV:VC:3], ALU.mult))
                dve.tensor_tensor(tile, tile, cfac[:, t, :].unsqueeze(2).broadcast_to(wide), ALU.mult).then_inc(s_cf, 1)
            minima(1)
            scales(0)
            for u in range(2, 18):
                if u < 16:
                    minima(u)
                if u - 1 < 16:
                    scales(u - 1)
                copies(u - 2)
            for d in range(KC):
                b = sg[:, d % 2]
                dve.wait_ge(s_sig, 3 * d + 3)
                dve.wait_ge(s_dm, 5 * d + 4)
                dve.tensor_tensor(b[:, 0, :], b[:, 0, :], ps[(5 * d + 3) % 8][:, :], ALU.mult).then_inc(s_mix, 1)
                dve.wait_ge(s_dm, 5 * d + 5)
                dve.tensor_tensor(b[:, 2, :], b[:, 2, :], ps[(5 * d + 4) % 8][:, :], ALU.mult).then_inc(s_mix, 1)
                dve.wait_ge(s_mix, 4 * d + 2)
                dve.tensor_tensor(b[:, 2, :], b[:, 2, :], b[:, 1, :], ALU.mult).then_inc(s_mix, 1)
                dve.wait_ge(s_mix, 4 * d + 3)
                dve.tensor_tensor(mixT[:, d, :], b[:, 0, :], b[:, 2, :], ALU.add).then_inc(s_mix, 1)

            dve.memset(rw[:, KC * RC:KC * RC + 24], 0.0).then_inc(s_pad, 1)

            def norm_stats(t, x, var_sem):
                for h in range(2):
                    put(dve.bn_stats(lnst[:, 40 + 6 * h:46 + 6 * h], x[:, h * 512:(h + 1) * 512]))
                dve.wait_ge(s_dve, n_dve[0])
                link(dve.bn_aggr(lnst[:, 8 * t:8 * t + 2], lnst[:, 40:52]))
                dve.tensor_scalar(lnst[:, 8 * t + 1:8 * t + 2], lnst[:, 8 * t + 1:8 * t + 2], EPS, None, ALU.add).then_inc(var_sem, 1)

            def normalise(t, out, x, std_sem, done):
                dve.wait_ge(std_sem, t + 1)
                link(dve.reciprocal(lnst[:, 36 + t:37 + t], lnst[:, 32 + t:33 + t]))
                link(dve.tensor_scalar(out, x, lnst[:, 8 * t:8 * t + 1], lnst[:, 36 + t:37 + t], ALU.subtract, ALU.mult))
                link(tt(out, out, ln1g, ALU.mult))
                tt(out, out, ln1b, ALU.add).then_inc(done, 1)

            def router_row(t):
                dve.wait_ge(s_lgm, t + 1)
                dve.tensor_tensor(lg[:, t, :], ps[2 * t][:, 0:RC], rrow, ALU.add).then_inc(s_lg, 1)

            dve.wait_ge(s_xr, 16)
            for t in range(TT):
                dve.wait_ge(s_womm, t + 1)
                for h in range(2):
                    x = x1t[:, t, h * 512:(h + 1) * 512]
                    put(dve.scalar_tensor_tensor(x, x, ALPHA, ps[2 * t + h][:, :], ALU.mult, ALU.add))
                dve.wait_ge(s_dve, n_dve[0])
                norm_stats(t, x1t[:, t, :], s_var)
                if t == 0:
                    dve.wait_ge(s_lr, 32)
                normalise(t, x1t[:, t, :], x1t[:, t, :], s_std, s_ln1)
                if t >= 1:
                    router_row(t - 1)
            router_row(TT - 1)
            dve.wait_ge(s_lg, TT)
            g4 = lg[:, :, 0:NG]
            link(dve.tensor_reduce(r4[2][:, 0, :], g4, AX, ALU.max))
            dve.tensor_tensor(rt[0], g4, r4[2][:, 0, :].unsqueeze(2).broadcast_to([P, TT, NG]), ALU.subtract).then_inc(s_gd, 1)
            for t in range(TT):
                put(dve.max(rt[1][:, t, :], lg[:, t, 0:NG]))
            dve.wait_ge(s_dve, n_dve[0])
            for t in range(TT):
                put(dve.max_index(rtu[0][:, t, :], rt[1][:, t, :], lg[:, t, 0:NG]))
            dve.wait_ge(s_dve, n_dve[0])
            link(dve.tensor_copy(r4[3][:, 0, :], rtu[0][:, :, 0]))
            link(tt(rt[2], iota_e[:, 0:NG].unsqueeze(1).broadcast_to([P, TT, NG]),
                    r4[3][:, 0, :].unsqueeze(2).broadcast_to([P, TT, NG]), ALU.is_equal))
            link(dve.tensor_scalar(rt[2], rt[2], 1.0, NEG, ALU.subtract, ALU.mult))
            link(tt(em, lg[:, :, NG:RC].rearrange("p t (g e) -> p t g e", g=NG),
                    rt[2].unsqueeze(3).broadcast_to([P, TT, NG, EPG]), ALU.add))
            e2 = em.rearrange("p t g e -> p t (g e)")
            for t in range(TT):
                put(dve.max(rt[3][:, t, :], e2[:, t, :]))
            dve.wait_ge(s_dve, n_dve[0])
            for t in range(TT):
                put(dve.max_index(rtu[1][:, t, :], rt[3][:, t, :], e2[:, t, :]))
            dve.tensor_tensor(r4[1][:, 0, :], rt[3][:, :, 1], rt[3][:, :, 0], ALU.subtract).then_inc(s_gd, 1)
            dve.wait_ge(s_dve, n_dve[0])
            best = r4[4]
            link(dve.tensor_copy(best.rearrange("p k t -> p t k"), rtu[1][:, :, 0:2]))
            link(tt(pick, iota_e.unsqueeze(1).unsqueeze(1).broadcast_to([P, 2, TT, NE]),
                    best.unsqueeze(3).broadcast_to([P, 2, TT, NE]), ALU.is_equal))
            tt(both, pick[:, 0], pick[:, 1], ALU.add).then_inc(s_pick, 1)
            dve.wait_ge(s_ge, 1)
            link(dve.tensor_reduce(r4[5][:, 0, :], rt[0], AX, ALU.add))
            dve.wait_ge(s_ge, 2)
            link(dve.tensor_scalar(r4[6][:, 0, :], r4[1][:, 0, :], 1.0, None, ALU.add))
            link(tt(r4[6][:, 0, :], r4[6][:, 0, :], r4[5][:, 0, :], ALU.mult))
            link(dve.reciprocal(wts[:, 0, :], r4[6][:, 0, :]))
            link(tt(wts[:, 1, :], wts[:, 0, :], r4[1][:, 0, :], ALU.mult))
            dve.wait_ge(s_rank, 1)
            nbe = r4[0][0:NE, 0, :]
            link(dve.tensor_copy(nbe[:, 0:1], ps[5][0:NE, 0:1]))
            link(dve.tensor_scalar(rt[4][0:NE, 0, :], thr, nbe[:, 0:1], None, ALU.is_lt))
            link(dve.tensor_reduce(nbe[:, 2:3], rt[4][0:NE, 0, :], AX, ALU.add))
            dve.tensor_scalar(nbe[:, 1:2], nbe[:, 2:3], fcol, 0.0, ALU.subtract, ALU.max).then_inc(s_nb, 1)
            for k in range(2):
                link(tt(prod, ps[7][:, 0:TT * NE].rearrange("p (t e) -> p t e", t=TT), pick[:, k], ALU.mult))
                link(dve.tensor_reduce(r4[7][:, k, :], prod, AX, ALU.add))
            dve.wait_ge(s_st, 1)
            dve.wait_ge(s_nb, 1)
            link(dve.tensor_scalar(r4[8][0:NE, 0, 0:1], ps[4][0:NE, 0:1], float(FORCED), None, ALU.add))
            link(tt(r4[8][0:NE, 0, 1:2], r4[8][0:NE, 0, 0:1], nbe[:, 1:2], ALU.add))
            link(tt(r4[8][0:NE, 0, 2:3], r4[8][0:NE, 0, 0:1], fcol, ALU.subtract))
            put(dve.tensor_scalar(diag[0:NE, :], eye[0:NE, 0:NE], r4[8][0:NE, 0, 2:3], None, ALU.mult))
            first, w = ind[0:NE, 0:TBW], ind[0:NE, TBW:2 * TBW]
            link(dve.tensor_scalar(w, iota_b, r4[8][0:NE, 0, 0:1], ecol, ALU.is_ge, ALU.mult))
            link(dve.scalar_tensor_tensor(first, iota_b, r4[8][0:NE, 0, 1:2], w, ALU.is_lt, ALU.mult))
            link(tt(first, first, forced_b, ALU.add))
            dve.tensor_copy(first[:, MAXB:MAXB + 1], nbe[:, 1:2]).then_inc(s_base, 1)
            dve.wait_ge(s_ids, 1)
            link(dve.tensor_copy(idf, ps[3][0:1, 128:128 + TBW]))
            put(dve.tensor_scalar(ids[0:1, 0:MAXB], idf[:, 0:MAXB], float(P), None, ALU.mult))
            put(dve.tensor_copy(ids[0:1, MAXB:MAXB + 1], idf[:, MAXB:MAXB + 1]))
            link(dve.tensor_scalar(ids[0:1, MAXB + 1:MAXB + 2], idf[:, MAXB:MAXB + 1], float(FORCED - 1), None, ALU.add))
            dve.tensor_scalar(ids[0:1, MAXB + 1:MAXB + 2], ids[0:1, MAXB + 1:MAXB + 2], 3, None, ALU.bitwise_and).then_inc(s_idr, 1)
            for k in range(2):
                link(tt(prod, ps[3][:, 0:NE].unsqueeze(1).broadcast_to([P, TT, NE]), pick[:, k], ALU.mult))
                link(dve.tensor_reduce(r4[9][:, k, :], prod, AX, ALU.add))
            flat = lambda t: t.rearrange("p k t -> p (k t)")
            link(dve.tensor_copy(lo_u, flat(r4[7])))
            put(dve.tensor_scalar(hi_u, lo_u, 6, None, ALU.logical_shift_right))
            dve.wait_ge(s_dve, n_dve[0])
            link(dve.tensor_scalar(lo_u, lo_u, BLK - 1, None, ALU.bitwise_and))
            hi, lo, blk, m1, m2 = (flat(r4[j]) for j in (10, 11, 12, 13, 14))
            put(dve.tensor_copy(hi, hi_u))
            put(dve.tensor_copy(lo, lo_u))
            dve.wait_ge(s_dve, n_dve[0])
            put(tt(blk, flat(r4[9]), hi, ALU.add))
            put(dve.tensor_scalar(m1, hi, 0.5, None, ALU.is_lt))
            dve.wait_ge(s_dve, n_dve[0])
            link(dve.scalar_tensor_tensor(m1, flat(best), FORCED - 0.5, m1, ALU.is_lt, ALU.mult))
            link(tt(m2, flat(best), blk, ALU.subtract))
            link(tt(m2, m2, m1, ALU.mult))
            link(tt(blk, blk, m2, ALU.add))
            put(tt(hot_blk, iota_all.unsqueeze(1).broadcast_to([P, 8, TBW]), blk.unsqueeze(2).broadcast_to([P, 8, TBW]), ALU.is_equal))
            wide = [P, 8, P]
            link(tt(hot_slot, slot_row.unsqueeze(1).broadcast_to(wide), lo.unsqueeze(2).broadcast_to(wide), ALU.is_equal))
            tt(hot_slot, hot_slot, token_less.unsqueeze(2).broadcast_to(wide), ALU.mult).then_inc(s_slot, 1)
            dve.wait_ge(s_tbl, 1)
            sf = ind[:, 0:TBW]
            put(dve.tensor_scalar(sf, ps[6][:, 0:TBW], float(INVALID), None, ALU.add))
            link(dve.tensor_scalar(lt, ps[6][:, 0:TBW], float(INVALID), None, ALU.add))
            for h in range(2):
                r = slice(BLK * h, BLK * (h + 1))
                put(dve.tensor_scalar(gidx[r, :], lt.rearrange("p (j h) -> p j h", h=2)[r, :, h], INVALID | (L - 1), None, ALU.bitwise_and))
            dve.wait_ge(s_dve, n_dve[0])
            dve.tensor_scalar(sidx, sf, 2.0, jcol, ALU.mult, ALU.add).then_inc(s_idx, 1)

            def tokens(p, q):
                dve.wait_ge(s_xt, p + 1)
                if not isinstance(p, int) or p >= 2:
                    dve.wait_ge(s_gu, 2 * p - 2)
                for h in range(2):
                    c = dve.tensor_copy(xgT[q][:, 4 * h:4 * h + 4, :], ps[h][:, :].rearrange("p (c t) -> p c t", c=4))
                c.then_inc(s_xe, 1)

            def hidden(n, k):
                dve.wait_ge(s_silu, n + 1)
                if not isinstance(n, int) or n >= 2:
                    dve.wait_ge(s_ht, n - 1)
                dve.tensor_tensor(hb[k % 2], gs[k % 2], ps[2 + k % 2][:, P:2 * P], ALU.mult).then_inc(s_h, 1)

            def hidden_out(n, k):
                dve.wait_ge(s_ht, n + 1)
                if not isinstance(n, int) or n >= 2:
                    dve.wait_ge(s_dn, n - 1)
                dve.tensor_copy(hT[k % 2], ps[4 + k % 2][:, 0:P]).then_inc(s_he, 1)

            def step(i, k):
                n = 4 * i + k
                if not isinstance(n, int) or n >= 1:
                    hidden_out(n - 1, (k + 3) % 4)
                if k % 2 == 0:
                    tokens(2 * i + (k // 2 + 1), (k // 2 + 1) % 2)
                hidden(n, k)

            tokens(0, 0)
            for k in range(4):
                step(0, k)
            dve.wait_ge(s_idr, 1)
            extra = dve.value_load(ids[0:1, MAXB:MAXB + 1], min_val=0, max_val=MAXB - 1 - FORCED)
            last = dve.value_load(ids[0:1, MAXB + 1:MAXB + 2], min_val=0, max_val=3)
            with dve.Fori(1, MAXB // 4) as i:
                for k in range(4):
                    with dve.If(4 * i + (k - FORCED) < extra):
                        step(i, k)
            for k in range(4):
                with dve.If(last == k):
                    hidden_out(extra + (FORCED - 1), k)
            dve.wait_ge(s_row2, 32)
            dve.wait_ge(s_xs, 1)

            def combine(t):
                y0, y1 = yt[:, t, 0, :], yt[:, t, 1, :]
                dve.wait_ge(s_yt[t], 16)
                link(dve.scalar_tensor_tensor(y0, y0, wts[:, 0, t:t + 1], x1t[:, t, :], ALU.mult, ALU.add))
                link(dve.scalar_tensor_tensor(y0, y1, wts[:, 1, t:t + 1], y0, ALU.mult, ALU.add))
                norm_stats(t, y0, s_var2)

            def scales2(t):
                dve.wait_ge(s_std2, t + 1)
                link(dve.reciprocal(lnst[:, 36 + t:37 + t], lnst[:, 32 + t:33 + t]))
                dve.scalar_tensor_tensor(lnst[:, 52 + t:53 + t], lnst[:, 8 * t:8 * t + 1], -1.0, lnst[:, 36 + t:37 + t],
                                         ALU.mult, ALU.mult).then_inc(s_nrm, 1)

            for j in range(TT + 2):
                if j < TT:
                    combine(j)
                if 1 <= j <= TT:
                    scales2(j - 1)
                if j >= 2:
                    dve.wait_ge(s_hat, j - 1)
                    dve.tensor_tensor(yt[:, j - 2, 1, :], yt[:, j - 2, 1, :], ln1g, ALU.mult).then_inc(s_gain, 1)

        @block.gpsimd
        def _(pool):
            pool.dma_start(prm, a["s5_params"]).then_inc(s_prm, 16)
            pool.dma_start(onehot, a["dist_onehot"]).then_inc(s_oh, 16)
            pool.dma_start(rtbl, a["bias_tbl"]).then_inc(s_oh, 16)
            pool.dma_start(eye, a["eye"]).then_inc(s_const, 16)
            pool.dma_start(bcol, a["bias_cols"]).then_inc(s_const, 16)
            pool.dma_start(w2dup, a["w2dup"]).then_inc(s_const, 16)
            pool.dma_start(b2row, a["rows"][0:1, ROW_B2:ROW_B2 + HD].broadcast_to([P, HD])).then_inc(s_const, 16)
            pool.dma_start(post, a["pos_t"]).then_inc(s_const, 16)
            pool.dma_start(s5d, a["s5_d"]).then_inc(s_const, 16)
            pool.dma_start(eyeh, a["eyeh"]).then_inc(s_const, 16)
            pool.dma_start(vrow, a["rows"][0:1, ROW_V:ROW_V + VC].broadcast_to([P, VC])).then_inc(s_vrow, 16)
            pool.memset(bbz, 0.0).then_inc(s_zero, 1)
            pool.memset(kz, 0.0).then_inc(s_zero, 1)
            pool.memset(blkz, 0.0).then_inc(s_zero, 1)
            pool.memset(kcz, 0.0).then_inc(s_zero, 1)
            pool.memset(vcz, 0.0).then_inc(s_zero, 1)
            pool.memset(toep, 0.0).then_inc(s_zero, 1)
            pool.wait_ge(s_toep, 16 * 16)
            pool.memset(xz, 0.0).then_inc(s_xz0, 1)
            pool.wait_ge(s_y, 4)
            pool.memset(pc, 0.0).then_inc(s_pcz, 1)
            for t in range(TT):
                pool.wait_ge(s_cf, t + 1)
                tile = pc[:, t, :, 0:NCMP]
                pool.affine_select(out=tile, in_=tile, compare_op=ALU.is_ge, fill=0.0, base=t * P - (CB - 1),
                                   pattern=[[0, HEADS], [-CS, NCMP]], channel_multiplier=1).then_inc(s_cm, 1)
            pool.wait_ge(s_womm, TT)
            for b in range(2):
                pool.memset(xg[b], 0.0).then_inc(s_xg0, 1)
            pool.wait_ge(s_idx, 1)
            pool.wait_ge(s_x1d, 16 * TT)
            pool.wait_ge(s_xg0, 2)

            def column(table, n, rows):
                return table[0:rows, n:n + 1] if isinstance(n, int) else table[0:rows, bass.ds(n, 1)]

            def gather(p, q):
                if not isinstance(p, int) or p >= 2:
                    pool.wait_ge(s_g[q], 8 * p - 8 * q)
                pool.tensor_copy(gcol[q], column(gidx, p, P)).then_inc(s_gi, 1)
                pool.wait_ge(s_gi, p + 1)
                if not isinstance(p, int) or p >= 2:
                    pool.wait_ge(s_xt, p - 1)
                pool.nop().then_inc(s_gst, 1)
                pool.indirect_dma_start(xg[q], None, x1_dram, bass.IndirectOffsetOnAxis(gcol[q], 0),
                                        bounds_check=L - 1, oob_is_err=False).then_inc(s_g[q], 16)

            def scatter(n, k):
                if not isinstance(n, int) or n >= 4:
                    pool.wait_ge(s_sct[k], 4 * n - 4 * k)
                pool.tensor_copy(scol[k], column(sidx, n, P)).then_inc(s_si, 1)
                pool.wait_ge(s_si, n + 1)
                pool.wait_ge(s_ye, n + 1)
                pool.nop().then_inc(s_sst, 1)
                pool.indirect_dma_start(ye_dram, bass.IndirectOffsetOnAxis(scol[k], 0), yb[k], None,
                                        bounds_check=4 * L - 1, oob_is_err=False).then_inc(s_sct[k], 16)

            def step(i, k):
                n = 4 * i + k
                if k % 2 == 0:
                    gather(2 * i + (k // 2 + 3), (k // 2 + 1) % 2)
                if not isinstance(n, int) or n >= 1:
                    scatter(n - 1, (k + 3) % 4)

            for p in range(3):
                gather(p, p % 2)
            for k in range(4):
                step(0, k)
            pool.wait_ge(s_idr, 1)
            extra = pool.value_load(ids[0:1, MAXB:MAXB + 1], min_val=0, max_val=MAXB - 1 - FORCED)
            last = pool.value_load(ids[0:1, MAXB + 1:MAXB + 2], min_val=0, max_val=3)
            with pool.Fori(1, MAXB // 4) as i:
                for k in range(4):
                    with pool.If(4 * i + (k - FORCED) < extra):
                        step(i, k)
            for k in range(4):
                with pool.If(last == k):
                    scatter(extra + (FORCED - 1), k)
                    n = extra + (FORCED - 1)
                    for j in range(4):
                        pool.wait_ge(s_sct[j], 4 * n - 4 * k + 16 * (j <= k))
                    for q in range(2):
                        pool.wait_ge(s_g[q], 4 * n - 4 * k + 32 + 16 * (q == 0 and k >= 2))
            pool.nop().then_inc(s_moe, 1)
            pool.wait_ge(s_row2, 32)
            for t in range(TT):
                pool.wait_ge(s_gain, t + 1)
                pool.tensor_tensor(yt[:, t, 0, :], yt[:, t, 1, :], ln1b, ALU.add).then_inc(s_ln2, 1)


def arena_pair(region, sp, i):
    t = sp[i]
    return bass.AP(t.tensor, t.offset, [list(t.ap[0]), [1, 2 * GP]])


def pack(inp):
    f = lambda n: np.asarray(inp[n])
    c = np.ascontiguousarray
    x = f("x")[0]
    w = f("w_in")[0]
    kv0 = ATT
    tile_cols = [(ATT + 6 * KV + 3 * HEADS + P * i) for i in range(4)]
    tile_cols += [kv0, kv0 + KV, kv0 + 2 * KV, kv0 + 4 * KV] + [P * i for i in range(4)]
    part = lambda m: m.reshape(m.shape[0] // P, P, -1).transpose(1, 0, 2).reshape(P, -1)
    front = [part(w[:, o:o + P]) for o in tile_cols]
    for i in range(2):
        w1 = f("cmp_w1")[0, i].reshape(4, 8, HD, CH)
        for r in range(4):
            t = w1[r].transpose(1, 0, 2).reshape(HD, 8 * CH)
            front.append(np.concatenate([t, t], 0))
    gates = kv0 + 6 * KV
    vcols = np.r_[kv0 + 3 * KV:kv0 + 4 * KV, kv0 + 5 * KV:kv0 + 6 * KV, gates:gates + 3 * HEADS]
    moff = gates + 3 * HEADS + SW
    mid = []
    for d in range(KC):
        mid.append(np.concatenate([
            part(w[:, moff + P * d:moff + P * (d + 1)]), part(w[:, moff + D + P * d:moff + D + P * (d + 1)]),
            part(f("w_attn_up")[0][:, P * d:P * (d + 1)]), part(f("s5_w_val")[0][:, P * d:P * (d + 1)]),
            part(f("s5_w_gate")[0][:, P * d:P * (d + 1)])], 1))
    b = f("b_in")[0]
    cols = [b[o:o + P] for o in tile_cols]
    cols += [b[moff + D * m + P * d:moff + D * m + P * (d + 1)] for d in range(KC) for m in range(2)]
    cols += [f("s5_b_gate")[0][P * d:P * (d + 1)] for d in range(KC)]
    cols += [f("cmp_b1")[0, i] for i in range(2)]
    cols += [np.concatenate([f("cmp_b2")[0, i]] * 2) for i in range(2)]
    ws = f("cmp_w2")[0]
    w2dup = np.stack([np.concatenate([ws[i], ws[i]], 1) for i in range(2)], 1)
    rows = np.concatenate([b[vcols], f("router_b_group")[0], f("router_b_expert")[0], f("cmp_b2")[0, 1],
                           f("ln1_g")[0], f("ln1_b")[0], f("ln2_g")[0], f("ln2_b")[0]])[None]
    pos = f("cmp_pos")[0].transpose(2, 0, 1)
    pair = lambda m: m.reshape((GP, 2) + m.shape[1:])
    lam = lambda n: pair(f(n)[0]).transpose(1, 2, 0).reshape(P, GP)
    dt = np.repeat(f("s5_log_dt")[0].reshape(GP, 2).T, SP_, 0)
    bm = lambda n: pair(f(n)[0]).transpose(1, 2, 0, 3).reshape(P, GP * SH)
    cm = lambda n: pair(f(n)[0]).transpose(1, 3, 0, 2).reshape(P, GP * SH)
    s5 = np.concatenate([lam("s5_lambda_re"), lam("s5_lambda_im"), dt, bm("s5_b_re"), bm("s5_b_im"),
                         cm("s5_c_re"), cm("s5_c_im")], 1)
    s5d = pair(f("s5_d")[0]).transpose(1, 2, 0).reshape(32, GP)
    dist = np.arange(-L, L)
    n = np.maximum(dist, 0)
    big = BUCKETS // 2 + (np.log(np.maximum(n, 1).astype(np.float32) / (BUCKETS // 2))
                          / math.log(MAXDIST / (BUCKETS // 2)) * (BUCKETS - BUCKETS // 2)).astype(np.int32)
    bucket = np.where(n < BUCKETS // 2, n, np.minimum(big, BUCKETS - 1))
    oh = np.zeros((BUCKETS + 1, 2 * L), np.float32)
    oh[bucket[dist >= 0], np.nonzero(dist >= 0)[0]] = -1.0
    oh[BUCKETS, dist < 0] = NEG
    onehot = np.concatenate([oh[:, ::-1], oh], 1)
    tbl = np.concatenate([f("rel_bias"), np.ones((1, HEADS), np.float32)], 0)
    wg, wu, wd = f("exp_w_gate")[0], f("exp_w_up")[0], f("exp_w_down")[0]
    gu = np.stack([wg.reshape(NE, KC, P, 2, P), wu.reshape(NE, KC, P, 2, P)], 4)
    gu = gu.transpose(0, 2, 1, 3, 4, 5).reshape(NE, P, KC * 2 * DE)
    dn = wd.reshape(NE, 2, P, D).transpose(0, 2, 1, 3).reshape(NE, P, 2 * D)
    experts = np.concatenate([gu, dn], 2).reshape(NE * P, EW)
    eyeh = np.tile(np.eye(SH, dtype=np.float32), (2, 1))
    router = part(np.concatenate([f("router_w_group")[0], f("router_w_expert")[0]], 1))
    ix = np.arange
    rc = np.zeros((P, NRC), np.float32)
    rc[:, 0:P] = ix(P)[:, None] < ix(P)[None]
    rc[:, P:2 * P] = 1.0
    rc[:, 2 * P:2 * P + NE] = ix(NE)
    o = 2 * P + NE
    rc[:, o:o + TBW] = ix(TBW)
    o += TBW
    for e in range(FORCED):
        rc[e, o + e] = e
    o += TBW
    rc[:, o] = ix(P)
    rc[:FORCED, o + 1] = 1.0
    rc[:, o + 2:o + 10] = BLK * ix(8)
    rc[BLK:, o + 10] = 1.0
    rc[:, o + 11:o + 19] = (ix(P)[:, None, None] + P * ix(TT)[None, None] + L * ix(2)[None, :, None]).reshape(P, 8) - INVALID
    rc[:, o + 19:o + 19 + P] = ix(P) % BLK
    out = {
        "route_consts": rc,
        "x_t": part(x.T), "x_rows": part(x), "front_w": np.stack(front), "w_v": part(w[:, vcols]),
        "mid_w": np.stack(mid), "w_out": part(f("w_out")[0]), "bias_cols": np.stack(cols, 1), "w2dup": w2dup.reshape(P, -1),
        "rows": rows, "pos_t": np.concatenate([pos, pos], 0).reshape(P, -1), "s5_params": s5, "s5_d": s5d,
        "dist_onehot": onehot, "bias_tbl": tbl, "eye": np.eye(P, dtype=np.float32), "eyeh": eyeh,
        "router_w": router, "experts": experts,
    }
    return {k: c(v) for k, v in out.items()}


def kernel(**inputs):
    import concourse.bacc as bacc
    from concourse.bass_utils import run_bass_kernel_spmd

    arrays = pack(inputs)
    nc = bacc.Bacc("TRN2", target_bir_lowering=False, num_devices=1)
    a = {n: nc.dram_tensor(n, v.shape, mybir.dt.from_np(v.dtype), kind="ExternalInput").ap() for n, v in arrays.items()}
    a["out"] = nc.dram_tensor("out", (L, D), F32, kind="ExternalOutput").ap()
    build_kernel(nc, a)
    result = run_bass_kernel_spmd(nc, [arrays], core_ids=[0])
    return np.asarray(result.results[0]["out"]).reshape(1, L, D)
```
